# Optimizing a Trainium2 kernel written in Bass

```python
import math
import jax
import jax.numpy as jnp
from jax import lax
import numpy as np

'''Hybrid chunk-causal encoder trunk with parallel head groups (DEPTH layers).

Input  x: (BATCH, SEQ, D_MODEL) float32.  Output: (BATCH, SEQ, D_MODEL).
Per layer:
  xn  = RMSNorm(x)
  p   = xn @ W_in  (one combined projection; columns split among three head groups)
  A   = differential attention heads (QK-norm, ALiBi, block-causal chunk mask)
  B   = stick-breaking attention heads (strictly causal, no positional encoding)
  C   = forgetting attention heads (QK-norm, data-dependent cumulative log-forget bias)
  h   = x + concat_heads(A, B, C) @ W_out
  y   = h + MoE(RMSNorm(h)), router shared by all layers, group-limited top-2 routing
'''

D_MODEL = 2048
BATCH = 1
SEQ = 256
DEPTH = 2

CHUNK = 64
Q_BLOCK = 128
HEAD_DIM = 128
N_HEADS = D_MODEL // HEAD_DIM
H_SB = N_HEADS // 3
H_FOX = N_HEADS // 3
H_DIFF = N_HEADS - H_SB - H_FOX
MIX_WIDTH = N_HEADS * HEAD_DIM
DIFF_HALF = HEAD_DIM // 2
N_IN = 3 * MIX_WIDTH + H_FOX
N_EXPERTS = 16
N_GROUPS = 4
EXPERTS_PER_GROUP = N_EXPERTS // N_GROUPS
TOP_K = 2
D_EXPERT = D_MODEL // 4
EPS = 1e-6

kernel_name = 'hybrid_diff_sb_fox_groupmoe_trunk'

def _split_points():
    wa, wb, wc = H_DIFF * HEAD_DIM, H_SB * HEAD_DIM, H_FOX * HEAD_DIM
    widths = [wa, wa, wa, wb, wb, wb, wc, wc, wc]
    pts, acc = [], 0
    for w in widths:
        acc += w
        pts.append(acc)
    return pts

def rms_norm(x, g):
    xf = x.astype(jnp.float32)
    y = xf * lax.rsqrt(jnp.mean(xf * xf, axis=-1, keepdims=True) + EPS)
    return (y * g.astype(jnp.float32)).astype(x.dtype)

def to_heads(t, n_heads, d):
    b, s, _ = t.shape
    return t.reshape(b, s, n_heads, d).transpose(0, 2, 1, 3)

def from_heads(t):
    b, h, s, d = t.shape
    return t.transpose(0, 2, 1, 3).reshape(b, s, h * d)

def _to_blocks(t):
    b, h, s = t.shape[:3]
    t = t.reshape((b, h, s // Q_BLOCK, Q_BLOCK) + t.shape[3:])
    return jnp.moveaxis(t, 2, 0)

def _from_blocks(o):
    o = jnp.moveaxis(o, 0, 2)
    b, h, nb, qb, d = o.shape
    return o.reshape(b, h, nb * qb, d)

def diff_attention(q1, q2, k1, k2, v, lam, slopes):
    seq = k1.shape[2]
    kpos = jnp.arange(seq)
    scale = DIFF_HALF ** -0.5

    def block(args):
        q1b, q2b, start = args
        qpos = start + jnp.arange(Q_BLOCK)
        allowed = (kpos[None, :] // CHUNK) <= (qpos[:, None] // CHUNK)
        dist = jnp.abs(qpos[:, None] - kpos[None, :]).astype(jnp.float32)
        bias = jnp.where(allowed[None], -slopes[:, None, None] * dist[None], -jnp.inf)
        s1 = jnp.einsum('bhqd,bhkd->bhqk', q1b, k1).astype(jnp.float32) * scale + bias
        s2 = jnp.einsum('bhqd,bhkd->bhqk', q2b, k2).astype(jnp.float32) * scale + bias
        w = jax.nn.softmax(s1, axis=-1) - lam * jax.nn.softmax(s2, axis=-1)
        return jnp.einsum('bhqk,bhkd->bhqd', w.astype(v.dtype), v)

    starts = jnp.arange(seq // Q_BLOCK) * Q_BLOCK
    return _from_blocks(lax.map(block, (_to_blocks(q1), _to_blocks(q2), starts)))

def stick_breaking_attention(q, k, v):
    seq = k.shape[2]
    kpos = jnp.arange(seq)
    scale = HEAD_DIM ** -0.5

    def block(args):
        qb, start = args
        qpos = start + jnp.arange(Q_BLOCK)
        strict = kpos[None, :] < qpos[:, None]
        z = jnp.einsum('bhqd,bhkd->bhqk', qb, k).astype(jnp.float32) * scale
        log_keep = jnp.where(strict, jax.nn.log_sigmoid(-z), 0.0)
        between = lax.cumsum(log_keep, axis=3, reverse=True) - log_keep
        a = jnp.where(strict, jnp.exp(jax.nn.log_sigmoid(z) + between), 0.0)
        return jnp.einsum('bhqk,bhkd->bhqd', a.astype(v.dtype), v)

    starts = jnp.arange(seq // Q_BLOCK) * Q_BLOCK
    return _from_blocks(lax.map(block, (_to_blocks(q), starts)))

def forgetting_attention(q, k, v, dcum):
    seq = k.shape[2]
    kpos = jnp.arange(seq)
    scale = HEAD_DIM ** -0.5

    def block(args):
        qb, dq, start = args
        qpos = start + jnp.arange(Q_BLOCK)
        causal = kpos[None, :] <= qpos[:, None]
        logits = jnp.einsum('bhqd,bhkd->bhqk', qb, k).astype(jnp.float32) * scale
        logits = logits + dq[..., :, None] - dcum[:, :, None, :]
        logits = jnp.where(causal, logits, -jnp.inf)
        p = jax.nn.softmax(logits, axis=-1)
        return jnp.einsum('bhqk,bhkd->bhqd', p.astype(v.dtype), v)

    starts = jnp.arange(seq // Q_BLOCK) * Q_BLOCK
    return _from_blocks(lax.map(block, (_to_blocks(q), _to_blocks(dcum), starts)))

def moe_ffn(h, w_router, router_bias, wg, wu, wd):
    b, s, d = h.shape
    t = h.reshape(b * s, d)
    scores = jax.nn.sigmoid((t @ w_router).astype(jnp.float32))
    sel = scores + router_bias.astype(jnp.float32)
    grp = sel.reshape(-1, N_GROUPS, EXPERTS_PER_GROUP)
    group_score = lax.top_k(grp, TOP_K)[0].sum(-1)
    best_group = jnp.argmax(group_score, axis=-1)
    in_group = (jnp.arange(N_EXPERTS) // EXPERTS_PER_GROUP)[None, :] == best_group[:, None]
    _, idx = lax.top_k(jnp.where(in_group, sel, -jnp.inf), TOP_K)
    gate = jnp.take_along_axis(scores, idx, axis=-1)
    gate = gate / jnp.sum(gate, axis=-1, keepdims=True)
    combine = jnp.sum(jax.nn.one_hot(idx, N_EXPERTS, dtype=jnp.float32) * gate[..., None], axis=1)
    hg = jnp.einsum('nd,edf->nef', t, wg)
    hu = jnp.einsum('nd,edf->nef', t, wu)
    act = jax.nn.silu(hg) * hu * combine[:, :, None].astype(t.dtype)
    out = jnp.einsum('nef,efd->nd', act, wd)
    return out.reshape(b, s, d)

def setup_inputs(seed: int = 0) -> dict:
    key = jax.random.key(seed)
    ks = jax.random.split(key, 24)
    f32 = jnp.float32
    nrm = lambda k, shape, sc: jax.random.normal(k, shape, f32) * sc
    gain = lambda k, shape: 1.0 + 0.02 * jax.random.normal(k, shape, f32)
    res_scale = (2.0 * DEPTH) ** -0.5
    return {
        'x': jax.random.normal(ks[0], (BATCH, SEQ, D_MODEL), f32),
        'attn_norm': gain(ks[1], (DEPTH, D_MODEL)),
        'w_in': nrm(ks[2], (DEPTH, D_MODEL, N_IN), D_MODEL ** -0.5),
        'b_forget': jax.random.uniform(ks[3], (DEPTH, H_FOX), f32, 1.0, 6.0),
        'qnorm_diff': gain(ks[4], (DEPTH, DIFF_HALF)),
        'knorm_diff': gain(ks[5], (DEPTH, DIFF_HALF)),
        'lam_q1': nrm(ks[6], (DEPTH, DIFF_HALF), 0.1),
        'lam_k1': nrm(ks[7], (DEPTH, DIFF_HALF), 0.1),
        'lam_q2': nrm(ks[8], (DEPTH, DIFF_HALF), 0.1),
        'lam_k2': nrm(ks[9], (DEPTH, DIFF_HALF), 0.1),
        'subln_diff': gain(ks[10], (DEPTH, HEAD_DIM)),
        'onorm_sb': gain(ks[11], (DEPTH, HEAD_DIM)),
        'qnorm_fox': gain(ks[12], (DEPTH, HEAD_DIM)),
        'knorm_fox': gain(ks[13], (DEPTH, HEAD_DIM)),
        'onorm_fox': gain(ks[14], (DEPTH, HEAD_DIM)),
        'w_out': nrm(ks[15], (DEPTH, MIX_WIDTH, D_MODEL), MIX_WIDTH ** -0.5 * res_scale),
        'ffn_norm': gain(ks[16], (DEPTH, D_MODEL)),
        'w_router': nrm(ks[17], (D_MODEL, N_EXPERTS), D_MODEL ** -0.5),
        'router_bias': nrm(ks[18], (N_EXPERTS,), 0.01),
        'w_gate': nrm(ks[19], (DEPTH, N_EXPERTS, D_MODEL, D_EXPERT), D_MODEL ** -0.5),
        'w_up': nrm(ks[20], (DEPTH, N_EXPERTS, D_MODEL, D_EXPERT), D_MODEL ** -0.5),
        'w_down': nrm(ks[21], (DEPTH, N_EXPERTS, D_EXPERT, D_MODEL), D_EXPERT ** -0.5 * res_scale),
    }

def reference(x, attn_norm, w_in, b_forget, qnorm_diff, knorm_diff, lam_q1, lam_k1, lam_q2, lam_k2,
              subln_diff, onorm_sb, qnorm_fox, knorm_fox, onorm_fox, w_out, ffn_norm,
              w_router, router_bias, w_gate, w_up, w_down):
    b, s, _ = x.shape
    slopes = jnp.exp2(-8.0 * jnp.arange(1, H_DIFF + 1, dtype=jnp.float32) / H_DIFF)
    pts = _split_points()
    for l in range(DEPTH):
        xn = rms_norm(x, attn_norm[l])
        proj = xn @ w_in[l]
        qa, ka, va, qb, kb, vb, qc, kc, vc, fc = jnp.split(proj, pts, axis=-1)

        qa = rms_norm(qa.reshape(b, s, H_DIFF, 2, DIFF_HALF).transpose(0, 2, 1, 3, 4), qnorm_diff[l])
        ka = rms_norm(ka.reshape(b, s, H_DIFF, 2, DIFF_HALF).transpose(0, 2, 1, 3, 4), knorm_diff[l])
        lam_init = 0.8 - 0.6 * math.exp(-0.3 * l)
        lam = (jnp.exp(jnp.sum(lam_q1[l].astype(jnp.float32) * lam_k1[l].astype(jnp.float32)))
               - jnp.exp(jnp.sum(lam_q2[l].astype(jnp.float32) * lam_k2[l].astype(jnp.float32)))
               + lam_init)
        oa = diff_attention(qa[..., 0, :], qa[..., 1, :], ka[..., 0, :], ka[..., 1, :],
                            to_heads(va, H_DIFF, HEAD_DIM), lam, slopes)
        oa = rms_norm(oa, subln_diff[l]) * (1.0 - lam_init)

        ob = stick_breaking_attention(to_heads(qb, H_SB, HEAD_DIM), to_heads(kb, H_SB, HEAD_DIM),
                                      to_heads(vb, H_SB, HEAD_DIM))
        ob = rms_norm(ob, onorm_sb[l])

        log_f = jax.nn.log_sigmoid((fc + b_forget[l]).astype(jnp.float32))
        dcum = jnp.cumsum(log_f, axis=1).transpose(0, 2, 1)
        oc = forgetting_attention(rms_norm(to_heads(qc, H_FOX, HEAD_DIM), qnorm_fox[l]),
                                  rms_norm(to_heads(kc, H_FOX, HEAD_DIM), knorm_fox[l]),
                                  to_heads(vc, H_FOX, HEAD_DIM), dcum)
        oc = rms_norm(oc, onorm_fox[l])

        mixed = jnp.concatenate([from_heads(oa), from_heads(ob), from_heads(oc)], axis=-1)
        x = x + mixed @ w_out[l]
        x = x + moe_ffn(rms_norm(x, ffn_norm[l]), w_router, router_bias, w_gate[l], w_up[l], w_down[l])
    return x


_drawn_inputs = setup_inputs


def setup_inputs(seed=0):
    import zlib

    import numpy as np

    out = dict(_drawn_inputs(seed))
    spreads = {}
    factors = {}
    for name, (base, spread) in spreads.items():
        noise = np.random.default_rng([zlib.crc32(name.encode()), seed]).standard_normal(out[name].shape)
        drawn = base * np.exp(spread * noise) if base else spread * noise
        out[name] = jnp.asarray(drawn.astype(out[name].dtype))
    for name, factor in factors.items():
        out[name] = (out[name] * factor).astype(out[name].dtype)
    return out
```

```python
from contextlib import ExitStack, contextmanager

import numpy as np

import concourse.bass as bass
from concourse import mybir

F32 = mybir.dt.float32
F32R = mybir.dt.float32r
I32 = mybir.dt.int32
U32 = mybir.dt.uint32
ALU = mybir.AluOpType
ACT = mybir.ActivationFunctionType
AX = mybir.AxisListType.X

P = 128
D, SEQ, DEPTH = 2048, 256, 2
NT = SEQ // P
NC = D // P
HD = 128
NH = D // HD
HB = HC = NH // 3
HA = NH - HB - HC
WIN = 3 * D
FPAD = HC + 1
NE, NG, F = 16, 4, D // 4
EG = NE // NG
EPS = 1e-6
SLOTS = P
BIG = 1e30
NOWHERE = 1048576.0

COLS = 512
UNIT = 4 * COLS
HALF = UNIT // 2
IN_UNITS = WIN * D // (P * UNIT)
OUT_UNITS = D * D // (P * UNIT)
EXP_UNITS = 3 * D * F // (P * UNIT)
NBLOCKS = (IN_UNITS + OUT_UNITS) // 4
RAW = 4
CUT = 4

QA, KA, VA = 0, HA * HD, 2 * HA * HD
QB, KB, VB = 3 * HA * HD, (3 * HA + HB) * HD, (3 * HA + 2 * HB) * HD
QC = 3 * (HA + HB) * HD
KC, VC = QC + HC * HD, QC + 2 * HC * HD
HEADS = [(g, i) for i in range(HA) for g in "abc" if i < {"a": HA, "b": HB, "c": HC}[g]]
QKV = {"a": (QA, KA, VA), "b": (QB, KB, VB), "c": (QC, KC, VC)}
MIX = {"a": 0, "b": HA, "c": HA + HB}
HALVES_A = 4 * HA
NORMS = HALVES_A + 2 * HC
SPAN = P + SEQ
ROWS = (slice(0, P), slice(P, SPAN))

SM = {}
_at = 0
for _name, _n in (("gqa", 1), ("gka", 1), ("gqc", 1), ("gkc", 1), ("goa", 1), ("gob", 1), ("goc", 1),
                  ("bf", HC), ("lam", 4 * 64), ("init", 1), ("rest", 1)):
    SM[_name] = (_at, _at + _n)
    _at += _n
SMALL = _at
CN = {}
_at = 0
for _name, _n in (("ident", P), ("before", P), ("ones", P), ("before2", P), ("upto", P), ("after", P),
                  ("ndist", SPAN), ("causal", P), ("slot", P), ("token", NT), ("gcode", NT * NG),
                  ("ecode", NT * NE), ("rbias", NE)):
    CN[_name] = (_at, _at + _n)
    _at += _n
CONST = _at


def shape_constants():
    t = np.zeros((P, CONST), np.float32)
    i, j = np.arange(P)[:, None], np.arange(P)[None, :]

    def put(name, v):
        t[:, CN[name][0]:CN[name][1]] = v

    put("ident", i == j)
    put("before", i < j)
    put("before2", i < j)
    put("ones", 1.0)
    put("upto", i <= j)
    put("after", i > j)
    q = np.concatenate([np.broadcast_to(i, (P, P)), np.broadcast_to(i + P, (P, SEQ))], 1)
    k = np.concatenate([np.arange(P), np.arange(SEQ)])[None, :]
    put("ndist", np.where(k // 64 <= q // 64, -np.abs(q - k), -BIG))
    put("causal", np.where(j <= i, 0.0, -BIG))
    put("slot", j)
    put("token", np.arange(P)[:, None] + P * np.arange(NT)[None, :] + 1)
    put("gcode", np.tile(NG - np.arange(NG), NT)[None, :])
    put("ecode", np.tile(NE - np.arange(NE), NT)[None, :])
    return t


FIXED = {
    "gain_landed": (32, 0), "small_landed": (32, 0), "rows_stored": (16 * NT, 0), "picks_landed": (32 * NT, 0),
    "x_ready": (2 * NT, 0), "rows_squared": (2, 0), "log_ready": (4, 0), "root_ready": (4, 0),
    "rows_ready": (2 * NT, 0), "gain_free": (1, 0), "t_banked": (3 * NC // 2, 0), "t_hi": (3 * NC // 2, 0),
    "t_lo": (3 * NC // 2, 0), "f_hi": (1, 0), "f_lo": (1, 0), "f_banked": (1, 0), "f_ready": (1, 0),
    "f_log": (1, 0), "logf_ready": (1, 0), "lam_dots": (1, 0), "lam_exp": (1, 0), "d_banked": (1, 0),
    "d_ready": (1, 0), "d_turned": (1, 0), "dT_ready": (1, 0), "sq_ready": (3 * NT, 0), "sq_read": (NT, 0),
    "head_norms": (1, 0), "q_banked": (NH, 0), "k_banked": (NH, 0), "qT_ready": (NH, 0),
    "kT_ready": (NH, 0), "s_banked": (NH, 0), "z_ready": (HB, 0), "nabs_ready": (HB, 0),
    "soft_ready": (HB, 0), "keep_ready": (HB, 0), "sum_ready": (HB, 0), "a_ready": (HB, 0),
    "aT_ready": (HB, 0), "neg_max": (HA + HC, 0), "exps_ready": (HA + HC, 0), "weights_ready": (HA, 0),
    "sums_ready": (HC, 0), "m_banked": (NH, 0), "wT_ready": (HA + HC, 0), "o_banked": (NH, 0),
    "o_ready": (NH, 0), "mix_scaled": (NT, 0), "r_banked": (1, 0), "r_exp": (1, 0), "mask_ready": (1, 0),
    "rank_banked": (1, 0), "block_out": (NBLOCKS, 0), "cut_free": (2 * (IN_UNITS + OUT_UNITS), 2 * NE * EXP_UNITS),
    "again_ready": (0, 1), "again_read": (0, 4), "chosen_ready": (0, NE), "slot_banked": (0, NE),
    "tables_ready": (0, 1),
}


class Tally:

    def __init__(self, e, sems, start=None, counted=()):
        self.e, self.sems = e, sems
        self.start = start or {}
        self.layer = 0
        self.rounds = e.alloc_register("rounds")
        e.reg_mov(self.rounds, 0)
        self.reg, self.base, self.n, self.in_round = {}, {}, {}, False
        for k in counted:
            self.reg[k] = e.alloc_register(f"seen_{k}")
            e.reg_mov(self.reg[k], self.start.get(k, 0))

    def due(self, k, n=1):
        e = self.e
        self.n[k] = self.n.get(k, 0) + n
        if k in self.reg:
            if k not in self.base:
                self.base[k] = e.snap(self.reg[k])
            value = self.base[k] + self.n[k]
        else:
            a, b = FIXED[k]
            value = self.start.get(k, 0) + self.n[k] + self.layer * a
            if b:
                if "rounds" not in self.base:
                    self.base["rounds"] = e.snap(self.rounds)
                value = value + self.base["rounds"] * b
        return value

    def fence(self):
        self.e.sem_inc(self.sems["fence"], 1)

    def by(self, k, n):
        return self.due(k, n - self.n.get(k, 0))

    def ahead(self, k, n):
        value = self.due(k, n)
        self.n[k] -= n
        return value

    def settle(self):
        for k, r in self.reg.items():
            if self.n.get(k):
                self.e.reg_add(r, r, self.n[k])
                self.n[k] = 0
        self.base.clear()

    @contextmanager
    def loop(self, cm):
        self.fence()
        self.settle()
        fixed = {k: n for k, n in self.n.items() if k not in self.reg}
        with cm as i:
            self.base.clear()
            yield i
            self.settle()
            now = {k: n for k, n in self.n.items() if k not in self.reg}
            assert all(n == fixed.get(k, 0) for k, n in now.items()), (fixed, now)

    @contextmanager
    def layers(self):
        with self.loop(self.e.Fori(0, DEPTH)) as layer:
            self.layer = layer
            yield layer
            self.layer = 0
            for k, n in self.n.items():
                if k not in self.reg:
                    assert n <= FIXED[k][0], (k, n)
                    self.n[k] = 0

    @contextmanager
    def one_round(self):
        e = self.e
        go = e.alloc_register("go")
        self.fence()
        e.reg_mov(go, 1)
        self.settle()
        with self.loop(e.While(lambda: e.snap(go))):
            before = dict(self.n)
            yield
            e.wait_ge(self.sems["again_ready"], self.due("again_ready"))
            self.fence()
            e.reg_mov(go, e.value_load(self.again, min_val=0, max_val=1))
            if self.tells:
                e.sem_inc(self.sems["again_read"], 1)
            for k in self.n:
                if k not in self.reg:
                    assert self.n[k] - before.get(k, 0) in (0, FIXED[k][1]), (k, self.n[k])
                    self.n[k] = before.get(k, 0)
            e.reg_add(self.rounds, self.rounds, 1)


def trunk(nc, x_in, in_units, forget_w, out_units, expert_units, norms, small_in, const_in, router_in,
          rows_dram, picks_dram, out):
    with ExitStack() as ctx:
        def sb(name, shape, dt=F32):
            return ctx.enter_context(nc.sbuf_tensor(name, shape, dt))

        def sem(name):
            return ctx.enter_context(nc.semaphore(name))

        bank = [ctx.enter_context(nc.psum_tensor(f"bank{i}", [P, COLS], F32)) for i in range(8)]

        x = sb("x", [P, NT, D])
        xh = sb("xh", [P, NC, SEQ], F32R)
        xl = sb("xl", [P, NC, SEQ], F32R)
        proj = sb("proj", [P, NT, WIN])
        rows = sb("rows", [P, NT, D])
        wide = sb("wide", [P, D])
        raw = sb("raw", [P, RAW, UNIT])
        wh = sb("wh", [P, CUT, HALF], F32R)
        wl = sb("wl", [P, CUT, HALF], F32R)
        const = sb("const", [P, CONST])
        small = sb("small", [P, SMALL])
        qkT = sb("qkT", [P, 2, 2, SEQ])
        wT = sb("wT", [P, 2, SPAN])
        actTh = sb("actTh", [P, F // P, SLOTS], F32R)
        actTl = sb("actTl", [P, F // P, SLOTS], F32R)
        fch = sb("fch", [P, NC, FPAD], F32R)
        fcl = sb("fcl", [P, NC, FPAD], F32R)
        fcr = sb("fcr", [P, NC, FPAD])
        rth = sb("rth", [P, NC, NE], F32R)
        rtl = sb("rtl", [P, NC, NE], F32R)
        stat = sb("stat", [P, 3, NT, NORMS])
        soft = sb("soft", [P, 3, 4, 4])
        logf = sb("logf", [P, 3, NT, HC])
        dcum = sb("dcum", [P, NT, HC])
        ndcT = sb("ndcT", [HC, SEQ])
        lam = sb("lam", [P, 4])
        more = sb("more", [1, 2])
        again = sb("again", [1, 1], I32)
        tok_at = sb("tok_at", [P, NE, 1], U32)
        put_at = sb("put_at", [P, NE, 1], U32)

        turned_qk = qkT[:, :, :, :].rearrange("p a b n -> p (a b n)")

        def table(at, width, form=None, **sizes):
            ap = turned_qk[:, at:at + width]
            return ap.rearrange(form, **sizes) if form else ap

        route = table(0, 8 * NT * NE, "p (k t n) -> p k t n", k=8, t=NT)
        pairs = table(256, 6 * NT * NG, "p (g n) -> p g n", n=6)
        few = table(304, 6 * NT * NG, "p (k g) -> p k g", k=6)
        info = table(352, 4 * NT * NE, "p (t n k) -> p t n k", t=NT, k=4)
        slots = table(480, 4 * NE, "p (n k) -> p n k", k=4)
        pick = table(544, 2 * NE, "p (k n) -> p k n", k=2)
        left = table(576, NE)

        def cst(name):
            return const[:, CN[name][0]:CN[name][1]]

        def sml(name):
            return small[:, SM[name][0]:SM[name][1]]

        ident, after, upto = cst("ident"), cst("after"), cst("upto")
        before, ones = cst("before"), cst("ones")
        strict = const[:, CN["before"][0]:CN["before2"][1]]
        score = wide[:, 0:4 * SPAN].rearrange("p (a b n) -> p a b n", a=2, b=2)
        chosen = wide[:, 0:4 * P].rearrange("p (a t n) -> p a t n", a=2, t=NT)
        router_raw = rows[:, 0, 0:NC * NE].rearrange("p (c n) -> p c n", c=NC)

        spare = proj[:, :, :].rearrange("p t n -> p (t n)")
        gathered = [spare[:, b * D:(b + 1) * D] for b in range(2)]
        expert_out = [spare[:, (2 + b) * D:(3 + b) * D] for b in range(2)]
        picked = gathered + expert_out
        act_tmp = spare[:, 4 * D:4 * D + F]
        act_rec = spare[:, 4 * D + F:4 * D + 2 * F]
        act = spare[:, 4 * D + 2 * F:4 * D + 3 * F]

        S = {n: sem(n) for n in (
            "start_landed x_landed out_stored router_ready hi_ready lo_ready cut_free block_out "
            "xt_banked xt_hi xt_lo sig_exp act_ready act_banked act_hi act_lo out_ready out_free "
            "act_done dve_done fence").split() + [k for k in FIXED if k not in ("cut_free", "block_out")]}
        for i in range(RAW):
            S[f"raw_landed{i}"] = sem(f"raw_landed{i}")
        for i in range(2):
            S[f"gather_landed{i}"] = sem(f"gather_landed{i}")
            S[f"scattered{i}"] = sem(f"scattered{i}")

        def tally(e, start=None, counted=(), tells=True):
            t = Tally(e, S, start, counted)
            t.again, t.tells = again[0:1, 0:1], tells
            return t

        block = ctx.enter_context(nc.Block())

        @block.sync
        def _(e):
            e.dma_start(const[:, :], const_in).then_inc(S["start_landed"], 16)
            e.dma_start(router_raw, router_in).then_inc(S["start_landed"], 16)
            for t in range(NT):
                e.dma_start(x[:, t, :], x_in[t * P:(t + 1) * P, :]).then_inc(S["x_landed"], 16)
            t_ = tally(e, counted=("lo_ready",))

            def load(units, at):
                for j in range(RAW):
                    e.wait_ge(S["lo_ready"], t_.due("lo_ready", 2))
                    e.dma_start(raw[:, j, :], units[bass.ds(at + j, 1)].rearrange("o p n -> (o p) n"))\
                        .then_inc(S[f"raw_landed{j}"], 16)

            with t_.layers() as layer:
                with t_.loop(e.Fori(0, IN_UNITS // RAW)) as i:
                    load(in_units, layer * IN_UNITS + i * RAW)
                with t_.loop(e.Fori(0, OUT_UNITS // RAW)) as i:
                    load(out_units, layer * OUT_UNITS + i * RAW)
                with t_.one_round():
                    with t_.loop(e.Fori(0, NE * EXP_UNITS // RAW)) as i:
                        load(expert_units, layer * (NE * EXP_UNITS) + i * RAW)
            e.wait_ge(S["x_ready"], NT * (2 * DEPTH + 1))
            for t in range(NT):
                e.dma_start(out[t * P:(t + 1) * P, :], x[:, t, :]).then_inc(S["out_stored"], 16)
            e.wait_ge(S["out_stored"], 16 * NT)

        @block.gpsimd
        def _(e):
            t_ = tally(e, start={"out_ready": 1},
                       counted=("xt_banked", "out_ready", "scattered0", "scattered1"))
            with t_.layers() as layer:
                e.dma_start(small[:, :], small_in[bass.ds(layer, 1)].rearrange("o p n -> (o p) n"))\
                    .then_inc(S["small_landed"], 16)
                e.dma_start(fcr[:, :, :], forget_w[bass.ds(layer, 1)].rearrange("o p c n -> (o p) c n"))\
                    .then_inc(S["small_landed"], 16)
                for k in range(2):
                    if k == 1:
                        e.wait_ge(S["gain_free"], t_.due("gain_free"))
                        t_.fence()
                    e.dma_start(wide[:, :], norms[bass.ds(layer * 2 + k, 1)].to_broadcast([P, D]))\
                        .then_inc(S["gain_landed"], 16)
                    e.wait_ge(S["rows_ready"], t_.due("rows_ready", NT))
                    t_.fence()
                for t in range(NT):
                    e.dma_start(rows_dram[t * P:(t + 1) * P, :], rows[:, t, :]).then_inc(S["rows_stored"], 16)
                e.wait_ge(S["rows_stored"], t_.due("rows_stored", 16 * NT))
                t_.fence()

                def gather(k):
                    e.indirect_dma_start(gathered[k % 2], None, rows_dram[:, :],
                                         bass.IndirectOffsetOnAxis(ap=tok_at[:, k % NE, :], axis=0),
                                         bounds_check=SEQ - 1, oob_is_err=False)\
                        .then_inc(S[f"gather_landed{k % 2}"], 16)

                def scatter(k):
                    e.wait_ge(S["out_ready"], t_.due("out_ready"))
                    t_.fence()
                    e.indirect_dma_start(picks_dram[:, :],
                                         bass.IndirectOffsetOnAxis(ap=put_at[:, k, :], axis=0),
                                         expert_out[k % 2], None,
                                         bounds_check=2 * SEQ - 1, oob_is_err=False)\
                        .then_inc(S[f"scattered{k % 2}"], 16)

                def freed(k):
                    e.wait_ge(S[f"scattered{k % 2}"], t_.due(f"scattered{k % 2}", 16))
                    t_.fence()
                    e.sem_inc(S["out_free"], 1)

                with t_.one_round():
                    e.wait_ge(S["tables_ready"], t_.due("tables_ready"))
                    t_.fence()
                    gather(0)
                    gather(1)
                    for k in range(NE):
                        e.wait_ge(S["xt_banked"], t_.due("xt_banked", 4))
                        t_.fence()
                        if k + 2 <= NE:
                            gather(k + 2)
                        if k >= 1:
                            if k >= 2:
                                freed(k - 2)
                            scatter(k - 1)
                    e.wait_ge(S["xt_banked"], t_.due("xt_banked", 4))
                    t_.fence()
                    freed(NE - 2)
                    scatter(NE - 1)
                    freed(NE - 1)
                for k in range(2 * NT):
                    e.dma_start(picked[k], picks_dram[k * P:(k + 1) * P, :]).then_inc(S["picks_landed"], 16)

        @block.scalar
        def _(e):
            act_ = nc.scalar.activation
            t_ = tally(e, start={"block_out": 2}, counted=(
                "cut_free", "raw_landed0", "raw_landed1", "raw_landed2", "raw_landed3",
                "xt_banked", "act_banked", "out_free", "act_done"))

            def cut(h):
                if h % 2 == 0:
                    e.wait_ge(S[f"raw_landed{h // 2 % RAW}"], t_.due(f"raw_landed{h // 2 % RAW}", 16))
                e.wait_ge(S["cut_free"], t_.due("cut_free"))
                act_(wh[:, h % CUT, :], raw[:, h // 2 % RAW, h % 2 * HALF:(h % 2 + 1) * HALF], ACT.Copy)\
                    .then_inc(S["hi_ready"], 1)

            def root(n):
                e.wait_ge(S["log_ready"], t_.due("log_ready"))
                act_(stat[:, 1, :, 0:n], stat[:, 0, :, 0:n], ACT.Ln).then_inc(S["act_done"], 1)
                e.wait_ge(S["act_done"], t_.due("act_done"))
                act_(stat[:, 1, :, 0:n], stat[:, 1, :, 0:n], ACT.Exp, scale=-0.5).then_inc(S["root_ready"], 1)

            def norm_rows():
                act_(rows[:, 0, :], x[:, 0, :], ACT.Square, accum_out=stat[:, 0, 0, 0:1])\
                    .then_inc(S["rows_squared"], 1)
                root(1)
                for g in range(NC // 2):
                    e.wait_ge(S["t_banked"], t_.due("t_banked"))
                    act_(xh[:, 2 * g:2 * g + 2, :], bank[4 + g % 4][:, :].rearrange("p (c n) -> p c n", c=2),
                         ACT.Copy).then_inc(S["t_hi"], 1)

            e.wait_ge(S["start_landed"], 32)
            act_(rth[:, :, :], router_raw, ACT.Copy).then_inc(S["router_ready"], 1)
            e.wait_ge(S["router_ready"], 2)
            e.wait_ge(S["x_landed"], 16 * NT)

            with t_.layers():
                e.wait_ge(S["x_ready"], t_.due("x_ready", NT))
                norm_rows()
                e.wait_ge(S["small_landed"], t_.due("small_landed", 32))
                act_(fch[:, :, :], fcr[:, :, :], ACT.Copy).then_inc(S["f_hi"], 1)
                e.wait_ge(S["lam_dots"], t_.due("lam_dots"))
                act_(lam[:, 0:2], lam[:, 0:2], ACT.Exp).then_inc(S["lam_exp"], 1)
                e.wait_ge(S["f_ready"], t_.due("f_ready"))
                act_(logf[:, 1, :, :], logf[:, 1, :, :], ACT.Exp).then_inc(S["act_done"], 1)
                e.wait_ge(S["act_done"], t_.due("act_done"))
                act_(logf[:, 1, :, :], logf[:, 1, :, :], ACT.Ln, bias=1.0).then_inc(S["f_log"], 1)

                with t_.loop(e.Fori(0, IN_UNITS // RAW)):
                    for h in range(2 * RAW):
                        cut(h)

                e.wait_ge(S["block_out"], t_.due("block_out", IN_UNITS // 4))
                for t in range(NT):
                    act_(rows[:, t, 0:HALVES_A * 64], proj[:, t, 0:HALVES_A * 64], ACT.Square)\
                        .then_inc(S["sq_ready"], 1)
                for t in range(NT):
                    e.wait_ge(S["sq_read"], t_.due("sq_read"))
                    act_(rows[:, t, 0:2 * HC * HD], proj[:, t, QC:QC + 2 * HC * HD], ACT.Square)\
                        .then_inc(S["sq_ready"], 1)
                root(NORMS)

                e.wait_ge(S["d_banked"], t_.due("d_banked"))
                act_(dcum[:, :, :], bank[6][:, 0:NT * HC].rearrange("p (t h) -> p t h", t=NT), ACT.Copy)\
                    .then_inc(S["d_ready"], 1)
                e.wait_ge(S["d_turned"], t_.due("d_turned"))
                act_(ndcT[:, :], bank[6][0:HC, 0:SEQ], ACT.Copy, scale=-1.0).then_inc(S["dT_ready"], 1)

                def query(i):
                    g, _ = HEADS[i]
                    e.wait_ge(S["q_banked"], t_.by("q_banked", i + 1))
                    scale = {"a": sml("gqa"), "b": float(HD) ** -0.5, "c": sml("gqc")}[g]
                    act_(qkT[:, i % 2, 0, :], bank[4][:, 0:SEQ], ACT.Copy, scale=scale)\
                        .then_inc(S["qT_ready"], 1)

                def scores(i):
                    g, _ = HEADS[i]
                    b = i % 2
                    if g == "b":
                        e.wait_ge(S["s_banked"], t_.by("s_banked", i + 1))
                        if i >= 2:
                            e.wait_ge(S["m_banked"], t_.by("m_banked", i - 1))
                        act_(score[:, b, 0, :], bank[2 * b][:, 0:SPAN], ACT.Copy).then_inc(S["z_ready"], 1)
                        e.wait_ge(S["nabs_ready"], t_.due("nabs_ready"))
                        act_(score[:, b, 1, :], score[:, b, 1, :], ACT.Exp).then_inc(S["act_done"], 1)
                        e.wait_ge(S["act_done"], t_.due("act_done"))
                        act_(score[:, b, 1, :], score[:, b, 1, :], ACT.Ln, bias=1.0)\
                            .then_inc(S["soft_ready"], 1)
                        return
                    e.wait_ge(S["neg_max"], t_.due("neg_max"))
                    for k in range(2 if g == "a" else 1):
                        for t, r in enumerate(ROWS):
                            c = 2 * t + k
                            last = act_(score[:, b, k, r], score[:, b, k, r], ACT.Exp,
                                        bias=soft[:, i % 3, 1, c:c + 1],
                                        accum_out=soft[:, i % 3, 2, c:c + 1])
                    last.then_inc(S["exps_ready"], 1)

                def turned(i):
                    g, _ = HEADS[i]
                    b = i % 2
                    if g == "b":
                        e.wait_ge(S["sum_ready"], t_.due("sum_ready"))
                        act_(score[:, b, 1, :], score[:, b, 1, :], ACT.Exp).then_inc(S["a_ready"], 1)
                        return
                    e.wait_ge(S["m_banked"], t_.by("m_banked", i + 1))
                    act_(wT[:, b, :], bank[6][:, 0:SPAN], ACT.Copy).then_inc(S["wT_ready"], 1)

                def output(i):
                    g, h = HEADS[i]
                    e.wait_ge(S["o_banked"], t_.by("o_banked", i + 1))
                    if g == "c":
                        e.wait_ge(S["sums_ready"], t_.due("sums_ready"))
                    at = (MIX[g] + h) * HD
                    for t in range(NT):
                        scale = soft[:, i % 3, 3, 2 * t:2 * t + 1] if g == "c" else 1.0
                        last = act_(rows[:, t, at:at + HD], bank[7][:, t * HD:(t + 1) * HD], ACT.Copy,
                                    scale=scale)
                    last.then_inc(S["o_ready"], 1)

                query(0)
                for i in range(NH + 2):
                    if i + 1 < NH:
                        query(i + 1)
                    if i < NH:
                        scores(i)
                    if i >= 2:
                        output(i - 2)
                    if 1 <= i <= NH:
                        turned(i - 1)

                e.wait_ge(S["o_ready"], t_.due("o_ready", NH))
                for t in range(NT):
                    act_(proj[:, t, 0:D], rows[:, t, :], ACT.Square).then_inc(S["sq_ready"], 1)
                root(NH)
                for g in range(NC // 2):
                    e.wait_ge(S["t_banked"], t_.due("t_banked"))
                    for c in (2 * g, 2 * g + 1):
                        gain = sml("goa" if c < HA else "gob" if c < HA + HB else "goc")
                        last = act_(xh[:, c, :], bank[4 + g % 4][:, c % 2 * SEQ:(c % 2 + 1) * SEQ], ACT.Copy,
                                    scale=gain)
                    last.then_inc(S["t_hi"], 1)

                with t_.loop(e.Fori(0, OUT_UNITS // RAW)):
                    for h in range(2 * RAW):
                        cut(h)

                e.wait_ge(S["x_ready"], t_.due("x_ready", NT))
                norm_rows()
                e.wait_ge(S["r_banked"], t_.due("r_banked"))
                act_(route[:, 0, :, :], bank[4][:, 0:NT * NE].rearrange("p (t n) -> p t n", t=NT), ACT.Exp,
                     scale=-1.0).then_inc(S["r_exp"], 1)

                def rows_hi(b):
                    for g in range(4):
                        e.wait_ge(S["xt_banked"], t_.due("xt_banked"))
                        act_(xh[:, 4 * g:4 * g + 4, b * P:(b + 1) * P],
                             bank[6 + g % 2][:, :].rearrange("p (c n) -> p c n", c=4), ACT.Copy)\
                            .then_inc(S["xt_hi"], 1)

                def store(b):
                    e.wait_ge(S["out_free"], t_.due("out_free"))
                    for k in range(4):
                        last = act_(expert_out[b][:, k * COLS:(k + 1) * COLS], bank[2 + k][:, :], ACT.Copy)
                    last.then_inc(S["out_ready"], 1)

                def expert(b, first=False):
                    for h in range(2 * EXP_UNITS):
                        cut(h)
                        if h == 3 and not first:
                            store(1 - b)
                        if h == 11:
                            act_(act_tmp, bank[0][:, :], ACT.Exp, scale=-1.0).then_inc(S["sig_exp"], 1)
                            rows_hi(1 - b)
                        if h == 19:
                            e.wait_ge(S["act_banked"], t_.due("act_banked"))
                            act_(actTh[:, :, :], bank[6][:, :].rearrange("p (c n) -> p c n", c=4), ACT.Copy)\
                                .then_inc(S["act_hi"], 1)

                with t_.one_round():
                    rows_hi(0)
                    expert(0, first=True)
                    expert(1)
                    with t_.loop(e.Fori(0, NE // 2 - 1)):
                        expert(0)
                        expert(1)
                    e.wait_ge(S["cut_free"], t_.ahead("cut_free", CUT))
                    store(1)

        @block.tensor
        def _(e):
            mm = nc.tensor.matmul
            t_ = tally(e, start={"lo_ready": 2 * RAW},
                       counted=("lo_ready", "block_out", "xt_lo", "act_ready", "act_lo", "out_ready",
                                "gather_landed0", "gather_landed1"))

            def three(out, at, tok, rh, rl, start, stop):
                mm(out, xh[:, at, tok], rh, start=start, stop=False)
                mm(out, xh[:, at, tok], rl, start=False, stop=False)
                return mm(out, xl[:, at, tok], rh, start=False, stop=stop)

            def turn_rows():
                for g in range(NC // 2):
                    if g >= 4:
                        e.wait_ge(S["t_lo"], t_.due("t_lo"))
                    for c in range(2):
                        for t in range(NT):
                            at = (2 * c + t) * P
                            last = e.transpose(bank[4 + g % 4][:, at:at + P],
                                               rows[:, t, (2 * g + c) * P:(2 * g + c + 1) * P], ident)
                    last.then_inc(S["t_banked"], 1)
                e.wait_ge(S["t_lo"], t_.due("t_lo", 4))

            def blocks():
                for b in range(2):
                    e.wait_ge(S["block_out"], t_.due("block_out"))
                    for h in range(2 * RAW):
                        e.wait_ge(S["lo_ready"], t_.due("lo_ready"))
                        for c in range(2):
                            k = slice(c * COLS, (c + 1) * COLS)
                            for t in range(NT):
                                last = three(bank[2 * b + t][:, :], 2 * h + c, slice(t * P, (t + 1) * P),
                                             wh[:, h % CUT, k], wl[:, h % CUT, k],
                                             h + c == 0, h == 2 * RAW - 1 and c == 1)
                        last.then_inc(S["cut_free"], 1)

            def turn(i):
                g, h = HEADS[i]
                for k, done in enumerate(("q_banked", "k_banked")):
                    at = QKV[g][k] + h * HD
                    for t in range(NT):
                        last = e.transpose(bank[4 + k][:, t * P:(t + 1) * P], proj[:, t, at:at + HD], ident)
                    last.then_inc(S[done], 1)

            def scores(i):
                g, h = HEADS[i]
                b = i % 2
                qT, kT = qkT[:, b, 0, :], qkT[:, b, 1, :]
                e.wait_ge(S["qT_ready"], t_.due("qT_ready"))
                e.wait_ge(S["kT_ready"], t_.due("kT_ready"))
                if g == "a":
                    for k in range(2):
                        half = slice(64 * k, 64 * k + 64)
                        for t, r in enumerate(ROWS):
                            last = mm(bank[2 * b + k][:, r], qT[half, t * P:(t + 1) * P],
                                      kT[half, 0:(t + 1) * P], start=True, stop=True)
                elif g == "b":
                    mm(bank[2 * b][:, 0:SEQ], kT[:, 0:P], qT[:, :], start=True, stop=True)
                    last = mm(bank[2 * b][:, SEQ:SPAN], kT[:, P:SEQ], qT[:, P:SEQ], start=True, stop=True)
                else:
                    for t, r in enumerate(ROWS):
                        mm(bank[2 * b][:, r], qT[:, t * P:(t + 1) * P], kT[:, 0:(t + 1) * P],
                           start=True, stop=False)
                        last = mm(bank[2 * b][:, r], ident[0:HC, h:h + 1].to_broadcast([HC, P]),
                                  ndcT[:, 0:(t + 1) * P], start=False, stop=True)
                last.then_inc(S["s_banked"], 1)

            def middle(i):
                g, _ = HEADS[i]
                b = i % 2
                if g == "b":
                    keep = score[:, b, 0, :]
                    e.wait_ge(S["keep_ready"], t_.due("keep_ready"))
                    mm(bank[6][:, 0:P], after, keep[:, 0:P], start=True, stop=True)
                    mm(bank[6][:, P:SEQ], after, keep[:, P:SEQ], start=True, stop=False)
                    mm(bank[6][:, P:SEQ], ones, keep[:, SEQ:SPAN], start=False, stop=True)
                    last = mm(bank[6][:, SEQ:SPAN], after, keep[:, SEQ:SPAN], start=True, stop=True)
                else:
                    e.wait_ge(S["exps_ready"], t_.due("exps_ready"))
                    if g == "a":
                        e.wait_ge(S["weights_ready"], t_.due("weights_ready"))
                    for k in range(3):
                        last = e.transpose(bank[6][:, k * P:(k + 1) * P], score[:, b, 0, k * P:(k + 1) * P],
                                           ident)
                last.then_inc(S["m_banked"], 1)

            def output(i):
                g, h = HEADS[i]
                b = i % 2
                at = QKV[g][2] + h * HD
                if g == "b":
                    e.wait_ge(S["aT_ready"], t_.due("aT_ready"))
                else:
                    e.wait_ge(S["wT_ready"], t_.due("wT_ready"))
                if i:
                    e.wait_ge(S["o_ready"], t_.due("o_ready"))
                mm(bank[7][:, 0:HD], wT[:, b, 0:P], proj[:, 0, at:at + HD], start=True, stop=True)
                for u in range(NT):
                    last = mm(bank[7][:, HD:2 * HD], wT[:, b, (1 + u) * P:(2 + u) * P],
                              proj[:, u, at:at + HD], start=(u == 0), stop=(u == 1))
                last.then_inc(S["o_banked"], 1)

            def turn_gathered(b):
                e.wait_ge(S[f"gather_landed{b}"], t_.due(f"gather_landed{b}", 16))
                for g in range(4):
                    if g >= 2:
                        e.wait_ge(S["xt_lo"], t_.due("xt_lo"))
                    for c in range(4):
                        at = (4 * g + c) * P
                        last = e.transpose(bank[6 + g % 2][:, c * P:(c + 1) * P],
                                           gathered[b][:, at:at + P], ident)
                    last.then_inc(S["xt_banked"], 1)

            def expert(b):
                tok = slice(b * P, (b + 1) * P)
                for m in range(2):
                    for h in range(8):
                        e.wait_ge(S["lo_ready"], t_.due("lo_ready"))
                        for c in range(2):
                            k = slice(c * COLS, (c + 1) * COLS)
                            last = three(bank[m][:, :], 2 * h + c, tok, wh[:, h % CUT, k],
                                         wl[:, h % CUT, k], h + c == 0, h == 7 and c == 1)
                        last.then_inc(S["cut_free"], 1)
                    if m == 0:
                        turn_gathered(1 - b)
                e.wait_ge(S["act_ready"], t_.due("act_ready"))
                e.wait_ge(S["xt_lo"], t_.due("xt_lo", 2))
                for k in range(F // P):
                    last = e.transpose(bank[6][:, k * P:(k + 1) * P], act[:, k * P:(k + 1) * P], ident)
                last.then_inc(S["act_banked"], 1)
                e.wait_ge(S["out_ready"], t_.due("out_ready"))
                e.wait_ge(S["act_lo"], t_.due("act_lo"))
                for h in range(8):
                    e.wait_ge(S["lo_ready"], t_.due("lo_ready"))
                    k = h // 2
                    for c in range(2):
                        r = slice(c * COLS, (c + 1) * COLS)
                        o = bank[2 + 2 * (h % 2) + c][:, :]
                        mm(o, actTh[:, k, :], wh[:, h % CUT, r], start=(k == 0), stop=False)
                        mm(o, actTh[:, k, :], wl[:, h % CUT, r], start=False, stop=False)
                        last = mm(o, actTl[:, k, :], wh[:, h % CUT, r], start=False, stop=(k == 3))
                    last.then_inc(S["cut_free"], 1)

            e.sem_inc(S["cut_free"], CUT)
            e.wait_ge(S["start_landed"], 32)
            e.wait_ge(S["router_ready"], 2)
            with t_.layers():
                e.wait_ge(S["rows_ready"], t_.due("rows_ready", NT))
                turn_rows()
                e.wait_ge(S["f_lo"], t_.due("f_lo"))
                for t in range(NT):
                    for c in range(NC):
                        last = three(bank[4][:, t * 8:t * 8 + FPAD], c, slice(t * P, (t + 1) * P),
                                     fch[:, c, :], fcl[:, c, :], c == 0, c == NC - 1)
                last.then_inc(S["f_banked"], 1)
                with t_.loop(e.Fori(0, IN_UNITS // RAW // 2)):
                    blocks()

                e.wait_ge(S["logf_ready"], t_.due("logf_ready"))
                for t in range(NT):
                    for u in range(t + 1):
                        last = mm(bank[6][:, t * HC:(t + 1) * HC], upto if u == t else ones, logf[:, 2, u, :],
                                  start=(u == 0), stop=(u == t))
                last.then_inc(S["d_banked"], 1)
                e.wait_ge(S["d_ready"], t_.due("d_ready"))
                for t in range(NT):
                    last = e.transpose(bank[6][0:HC, t * P:(t + 1) * P], dcum[:, t, :], ident)
                last.then_inc(S["d_turned"], 1)
                e.wait_ge(S["dT_ready"], t_.due("dT_ready"))
                e.wait_ge(S["head_norms"], t_.due("head_norms"))
                turn(0)
                for i in range(NH + 2):
                    if i < NH:
                        scores(i)
                    if i + 1 < NH:
                        turn(i + 1)
                    if i >= 2:
                        output(i - 2)
                    if 1 <= i <= NH:
                        middle(i - 1)
                e.wait_ge(S["o_ready"], t_.due("o_ready"))

                e.wait_ge(S["mix_scaled"], t_.due("mix_scaled", NT))
                turn_rows()
                with t_.loop(e.Fori(0, OUT_UNITS // RAW // 2)):
                    blocks()

                e.wait_ge(S["rows_ready"], t_.due("rows_ready", NT))
                turn_rows()
                for t in range(NT):
                    for c in range(NC):
                        last = three(bank[4][:, t * NE:(t + 1) * NE], c, slice(t * P, (t + 1) * P),
                                     rth[:, c, :], rtl[:, c, :], c == 0, c == NC - 1)
                last.then_inc(S["r_banked"], 1)
                e.wait_ge(S["mask_ready"], t_.due("mask_ready"))
                for t in range(NT):
                    for u in range(t + 1):
                        mm(bank[5][:, t * NE:(t + 1) * NE], before if u == t else ones, route[:, 7, u, :],
                           start=(u == 0), stop=(u == t))
                for t in range(NT):
                    last = mm(bank[5][:, NT * NE:(NT + 1) * NE], ones, route[:, 7, t, :],
                              start=(t == 0), stop=(t == NT - 1))
                last.then_inc(S["rank_banked"], 1)

                with t_.one_round():
                    for k in range(NE):
                        e.wait_ge(S["chosen_ready"], t_.due("chosen_ready"))
                        for t in range(NT):
                            last = mm(bank[6][:, 4 * k:4 * k + 4], chosen[:, k % 2, t, :], info[:, t, k, :],
                                      start=(t == 0), stop=(t == NT - 1))
                        last.then_inc(S["slot_banked"], 1)
                    e.wait_ge(S["tables_ready"], t_.due("tables_ready"))
                    turn_gathered(0)
                    e.wait_ge(S["xt_lo"], t_.due("xt_lo", 2))
                    with t_.loop(e.Fori(0, NE // 2)):
                        expert(0)
                        expert(1)

        @block.vector
        def _(e):
            v = nc.vector
            t_ = tally(e, start={"cut_free": CUT, "block_out": 2}, tells=False,
                       counted=("hi_ready", "xt_hi", "sig_exp", "act_hi", "act_banked", "dve_done"))

            def cut(h):
                e.wait_ge(S["hi_ready"], t_.due("hi_ready"))
                v.tensor_tensor(wl[:, h % CUT, :], raw[:, h // 2 % RAW, h % 2 * HALF:(h % 2 + 1) * HALF],
                                wh[:, h % CUT, :].bitcast(F32), ALU.subtract).then_inc(S["lo_ready"], 1)

            def blocks(n, empty):
                def one(behind):
                    for h in range(2 * RAW):
                        cut(h)
                        if h == 3 and behind is not None:
                            empty(*behind)
                one(None)
                with t_.loop(e.Fori(0, n // 2 - 1)) as i:
                    one((i * 2, 0))
                    one((i * 2 + 1, 1))
                one((n - 2, 0))
                e.wait_ge(S["cut_free"], t_.due("cut_free", 2 * RAW * n))
                empty(n - 1, 1)
                e.wait_ge(S["block_out"], t_.due("block_out", n))

            def refine(n, scale):
                for k, (a, b) in scale.items():
                    last = v.tensor_scalar(stat[:, 0, :, a:b], stat[:, 0, :, a:b], 1.0 / k, EPS,
                                           ALU.mult, ALU.add)
                last.then_inc(S["log_ready"], 1)
                e.wait_ge(S["root_ready"], t_.due("root_ready"))
                ms, y, r = stat[:, 0, :, 0:n], stat[:, 1, :, 0:n], stat[:, 2, :, 0:n]
                v.tensor_tensor(r, y, y, ALU.mult).then_inc(S["dve_done"], 1)
                e.wait_ge(S["dve_done"], t_.due("dve_done"))
                v.tensor_tensor(r, r, ms, ALU.mult).then_inc(S["dve_done"], 1)
                e.wait_ge(S["dve_done"], t_.due("dve_done"))
                v.tensor_scalar(r, r, -0.5, 1.5, ALU.mult, ALU.add).then_inc(S["dve_done"], 1)
                e.wait_ge(S["dve_done"], t_.due("dve_done"))
                v.tensor_tensor(r, r, y, ALU.mult).then_inc(S["dve_done"], 1)
                e.wait_ge(S["dve_done"], t_.due("dve_done"))

            def norm_rows():
                e.wait_ge(S["x_ready"], t_.due("x_ready", NT))
                e.wait_ge(S["gain_landed"], t_.due("gain_landed", 16))
                v.tensor_tensor_reduce(out=rows[:, 1, :], in0=x[:, 1, :], in1=x[:, 1, :], scale=1.0,
                                       scalar=0.0, op0=ALU.mult, op1=ALU.add,
                                       accum_out=stat[:, 0, 1, 0:1]).then_inc(S["dve_done"], 1)
                e.wait_ge(S["dve_done"], t_.due("dve_done"))
                e.wait_ge(S["rows_squared"], t_.due("rows_squared"))
                refine(1, {D: (0, 1)})
                for t in range(NT):
                    v.scalar_tensor_tensor(out=rows[:, t, :], in0=x[:, t, :], scalar=stat[:, 2, t, 0:1],
                                           in1=wide[:, :], op0=ALU.mult, op1=ALU.mult)\
                        .then_inc(S["rows_ready"], 1)
                for g in range(NC // 2):
                    e.wait_ge(S["t_hi"], t_.due("t_hi"))
                    k = slice(2 * g, 2 * g + 2)
                    v.tensor_tensor(xl[:, k, :], bank[4 + g % 4][:, :].rearrange("p (c n) -> p c n", c=2),
                                    xh[:, k, :].bitcast(F32), ALU.subtract).then_inc(S["t_lo"], 1)

            def scaled_heads(ap, r, n):
                view = ap.rearrange("p (h n) -> p h n", h=n)
                width = view.shape[2]
                return v.tensor_tensor(view, view, r.unsqueeze(2).to_broadcast([P, n, width]), ALU.mult)

            e.wait_ge(S["start_landed"], 32)
            e.wait_ge(S["router_ready"], 1)
            v.tensor_tensor(rtl[:, :, :], router_raw, rth[:, :, :].bitcast(F32), ALU.subtract)\
                .then_inc(S["router_ready"], 1)
            e.wait_ge(S["router_ready"], 2)
            e.wait_ge(S["x_landed"], 16 * NT)
            e.sem_inc(S["lo_ready"], 2 * RAW)
            e.sem_inc(S["block_out"], 2)
            e.sem_inc(S["x_ready"], NT)
            e.sem_inc(S["again_read"], 4)
            e.sem_inc(S["out_ready"], 1)
            e.sem_inc(S["out_free"], 2)

            with t_.layers():
                norm_rows()
                e.wait_ge(S["small_landed"], t_.due("small_landed", 32))
                e.wait_ge(S["f_hi"], t_.due("f_hi"))
                v.tensor_tensor(fcl[:, :, :], fcr[:, :, :], fch[:, :, :].bitcast(F32), ALU.subtract)\
                    .then_inc(S["f_lo"], 1)
                v.tensor_scalar(sml("gqa"), sml("gqa"), 64.0 ** -0.5, None, ALU.mult)
                v.tensor_scalar(sml("gqc"), sml("gqc"), float(HD) ** -0.5, None, ALU.mult)
                v.tensor_scalar(sml("goa"), sml("goa"), sml("rest"), None, ALU.mult)
                vec = sml("lam").rearrange("p (a n) -> p a n", a=4)
                scratch = slots[:, :, :].rearrange("p a b -> p (a b)")
                for k in range(2):
                    ins = v.tensor_tensor_reduce(out=scratch, in0=vec[:, 2 * k, :], in1=vec[:, 2 * k + 1, :],
                                                 scale=1.0, scalar=0.0, op0=ALU.mult, op1=ALU.add,
                                                 accum_out=lam[:, k:k + 1])
                    if k == 0:
                        ins.then_inc(S["dve_done"], 1)
                        e.wait_ge(S["dve_done"], t_.due("dve_done"))
                ins.then_inc(S["lam_dots"], 1)
                e.wait_ge(S["lam_exp"], t_.due("lam_exp"))
                v.tensor_tensor(lam[:, 2:3], lam[:, 0:1], lam[:, 1:2], ALU.subtract).then_inc(S["dve_done"], 1)
                e.wait_ge(S["dve_done"], t_.due("dve_done"))
                v.tensor_tensor(lam[:, 3:4], lam[:, 2:3], sml("init"), ALU.add).then_inc(S["dve_done"], 1)
                e.wait_ge(S["dve_done"], t_.due("dve_done"))
                e.wait_ge(S["f_banked"], t_.due("f_banked"))
                for t in range(NT):
                    ins = v.tensor_tensor(logf[:, 0, t, :], bank[4][:, t * 8:t * 8 + HC], sml("bf"), ALU.add)
                ins.then_inc(S["dve_done"], 1)
                e.wait_ge(S["dve_done"], t_.due("dve_done"))
                v.scalar_tensor_tensor(out=logf[:, 1, :, :], in0=logf[:, 0, :, :], scalar=-1.0,
                                       in1=logf[:, 0, :, :], op0=ALU.mult, op1=ALU.min)\
                    .then_inc(S["f_ready"], 1)
                e.wait_ge(S["f_log"], t_.due("f_log"))
                v.scalar_tensor_tensor(out=logf[:, 2, :, :], in0=logf[:, 0, :, :], scalar=0.0,
                                       in1=logf[:, 1, :, :], op0=ALU.min, op1=ALU.subtract)\
                    .then_inc(S["logf_ready"], 1)

                def to_proj(j, b):
                    for t in range(NT):
                        last = v.tensor_scalar(proj[:, t, bass.ds(j * COLS, COLS)], bank[2 * b + t][:, :],
                                               1.0, None, ALU.mult)
                    last.then_inc(S["block_out"], 1)

                blocks(IN_UNITS // 4, to_proj)

                for t in range(NT):
                    e.wait_ge(S["sq_ready"], t_.due("sq_ready"))
                    v.tensor_reduce(stat[:, 0, t, 0:HALVES_A],
                                    rows[:, t, 0:HALVES_A * 64].rearrange("p (h n) -> p h n", n=64), AX, ALU.add)\
                        .then_inc(S["sq_read"], 1)
                for t in range(NT):
                    e.wait_ge(S["sq_ready"], t_.due("sq_ready"))
                    ins = v.tensor_reduce(stat[:, 0, t, HALVES_A:NORMS],
                                          rows[:, t, 0:2 * HC * HD].rearrange("p (h n) -> p h n", n=HD),
                                          AX, ALU.add)
                ins.then_inc(S["dve_done"], 1)
                e.wait_ge(S["dve_done"], t_.due("dve_done"))
                refine(NORMS, {64: (0, HALVES_A), HD: (HALVES_A, NORMS)})
                for t in range(NT):
                    scaled_heads(proj[:, t, 0:HALVES_A * 64], stat[:, 2, t, 0:HALVES_A], HALVES_A)
                    ins = scaled_heads(proj[:, t, QC:QC + 2 * HC * HD], stat[:, 2, t, HALVES_A:NORMS], 2 * HC)
                ins.then_inc(S["head_norms"], 1)

                def key(i):
                    g, _ = HEADS[i]
                    e.wait_ge(S["k_banked"], t_.by("k_banked", i + 1))
                    gain = {"a": sml("gka"), "b": 1.0, "c": sml("gkc")}[g]
                    v.tensor_scalar(qkT[:, i % 2, 1, :], bank[5][:, 0:SEQ], gain, None, ALU.mult)\
                        .then_inc(S["kT_ready"], 1)

                def scores(i):
                    g, h = HEADS[i]
                    b, m = i % 2, i % 3
                    if i >= 2 and HEADS[i - 2][0] == "b":
                        e.wait_ge(S["aT_ready"], t_.by("aT_ready", HEADS[i - 2][1] + 1))
                    if g == "b":
                        z, w = score[:, b, 0, :], score[:, b, 1, :]
                        e.wait_ge(S["z_ready"], t_.due("z_ready"))
                        v.scalar_tensor_tensor(out=w, in0=z, scalar=-1.0, in1=z, op0=ALU.mult, op1=ALU.min)\
                            .then_inc(S["nabs_ready"], 1)
                        e.wait_ge(S["soft_ready"], t_.due("soft_ready"))
                        v.scalar_tensor_tensor(out=w, in0=z, scalar=0.0, in1=w, op0=ALU.min,
                                               op1=ALU.subtract).then_inc(S["dve_done"], 1)
                        e.wait_ge(S["dve_done"], t_.due("dve_done"))
                        v.tensor_tensor(z, w, z, ALU.subtract).then_inc(S["dve_done"], 1)
                        e.wait_ge(S["dve_done"], t_.due("dve_done"))
                        v.tensor_tensor(z, z, strict, ALU.mult).then_inc(S["keep_ready"], 1)
                        return
                    e.wait_ge(S["s_banked"], t_.by("s_banked", i + 1))
                    if i >= 2:
                        e.wait_ge(S["m_banked"], t_.by("m_banked", i - 1))
                    ns = 2 if g == "a" else 1
                    if g == "a":
                        slope = 2.0 ** (-8.0 * (h + 1) / HA)
                        for k in range(2):
                            ins = v.scalar_tensor_tensor(out=score[:, b, k, :], in0=cst("ndist"), scalar=slope,
                                                         in1=bank[2 * b + k][:, 0:SPAN], op0=ALU.mult, op1=ALU.add)
                    else:
                        s, lg = score[:, b, 0, :], bank[2 * b]
                        v.scalar_tensor_tensor(out=s[:, 0:P], in0=lg[:, 0:P], scalar=dcum[:, 0, h:h + 1],
                                               in1=cst("causal"), op0=ALU.add, op1=ALU.add)
                        v.tensor_scalar(s[:, P:2 * P], lg[:, P:2 * P], dcum[:, 1, h:h + 1], None, ALU.add)
                        ins = v.scalar_tensor_tensor(out=s[:, 2 * P:SPAN], in0=lg[:, 2 * P:SPAN],
                                                     scalar=dcum[:, 1, h:h + 1], in1=cst("causal"),
                                                     op0=ALU.add, op1=ALU.add)
                    ins.then_inc(S["dve_done"], 1)
                    e.wait_ge(S["dve_done"], t_.due("dve_done"))
                    for t, r in enumerate(ROWS):
                        ins = v.tensor_reduce(soft[:, m, 0, 2 * t:2 * t + ns], score[:, b, 0:ns, r], AX, ALU.max)
                    ins.then_inc(S["dve_done"], 1)
                    e.wait_ge(S["dve_done"], t_.due("dve_done"))
                    v.tensor_scalar(soft[:, m, 1, :] if g == "a" else soft[:, m, 1, 0:3:2],
                                    soft[:, m, 0, :] if g == "a" else soft[:, m, 0, 0:3:2],
                                    -1.0, None, ALU.mult).then_inc(S["neg_max"], 1)
                    e.wait_ge(S["exps_ready"], t_.due("exps_ready"))
                    if g == "c":
                        v.reciprocal(soft[:, m, 3, 0:3:2], soft[:, m, 2, 0:3:2]).then_inc(S["sums_ready"], 1)
                        return
                    v.reciprocal(soft[:, m, 3, :], soft[:, m, 2, :]).then_inc(S["dve_done"], 1)
                    e.wait_ge(S["dve_done"], t_.due("dve_done"))
                    v.tensor_scalar(soft[:, m, 3, 1:4:2], soft[:, m, 3, 1:4:2], lam[:, 3:4], None, ALU.mult)\
                        .then_inc(S["dve_done"], 1)
                    e.wait_ge(S["dve_done"], t_.due("dve_done"))
                    for t, r in enumerate(ROWS):
                        ins = v.tensor_scalar(score[:, b, 1, r], score[:, b, 1, r],
                                              soft[:, m, 3, 2 * t + 1:2 * t + 2], None, ALU.mult)
                    ins.then_inc(S["dve_done"], 1)
                    e.wait_ge(S["dve_done"], t_.due("dve_done"))
                    for t, r in enumerate(ROWS):
                        ins = v.scalar_tensor_tensor(out=score[:, b, 0, r], in0=score[:, b, 0, r],
                                                     scalar=soft[:, m, 3, 2 * t:2 * t + 1],
                                                     in1=score[:, b, 1, r], op0=ALU.mult, op1=ALU.subtract)
                    ins.then_inc(S["weights_ready"], 1)

                def turned(i):
                    g, _ = HEADS[i]
                    b = i % 2
                    if g != "b":
                        return
                    w = score[:, b, 1, :]
                    e.wait_ge(S["m_banked"], t_.by("m_banked", i + 1))
                    v.tensor_tensor(w, w, bank[6][:, 0:SPAN], ALU.add).then_inc(S["sum_ready"], 1)
                    e.wait_ge(S["a_ready"], t_.due("a_ready"))
                    if i >= 2:
                        e.wait_ge(S["o_banked"], t_.by("o_banked", i - 1))
                    v.tensor_tensor(wT[:, b, :], w, strict, ALU.mult).then_inc(S["aT_ready"], 1)

                key(0)
                for i in range(NH + 2):
                    if i + 1 < NH:
                        key(i + 1)
                    if i < NH:
                        scores(i)
                    if 1 <= i <= NH:
                        turned(i - 1)
                e.wait_ge(S["m_banked"], t_.by("m_banked", NH))
                e.sem_inc(S["gain_free"], 1)

                for t in range(NT):
                    e.wait_ge(S["sq_ready"], t_.due("sq_ready"))
                    ins = v.tensor_reduce(stat[:, 0, t, 0:NH],
                                          proj[:, t, 0:D].rearrange("p (h n) -> p h n", n=HD), AX, ALU.add)
                ins.then_inc(S["dve_done"], 1)
                e.wait_ge(S["dve_done"], t_.due("dve_done"))
                refine(NH, {HD: (0, NH)})
                for t in range(NT):
                    scaled_heads(rows[:, t, :], stat[:, 2, t, 0:NH], NH).then_inc(S["mix_scaled"], 1)
                for g in range(NC // 2):
                    e.wait_ge(S["t_hi"], t_.due("t_hi"))
                    for c in (2 * g, 2 * g + 1):
                        gain = sml("goa" if c < HA else "gob" if c < HA + HB else "goc")
                        last = v.scalar_tensor_tensor(out=xl[:, c, :],
                                                      in0=bank[4 + g % 4][:, c % 2 * SEQ:(c % 2 + 1) * SEQ],
                                                      scalar=gain, in1=xh[:, c, :].bitcast(F32),
                                                      op0=ALU.mult, op1=ALU.subtract)
                    last.then_inc(S["t_lo"], 1)

                def to_x(j, b):
                    for t in range(NT):
                        c = bass.ds(j * COLS, COLS)
                        last = v.tensor_tensor(x[:, t, c], bank[2 * b + t][:, :], x[:, t, c], ALU.add)
                    last.then_inc(S["block_out"], 1)

                blocks(OUT_UNITS // 4, to_x)
                e.sem_inc(S["x_ready"], NT)

                norm_rows()
                R = lambda k: route[:, k, :, :]
                G = lambda k: route[:, k, :, :].rearrange("p t (g n) -> p (t g) n", n=EG)

                def over(ap, n):
                    return ap.unsqueeze(2).to_broadcast([P, ap.shape[1], n])

                e.wait_ge(S["r_exp"], t_.due("r_exp"))
                v.tensor_scalar(R(0), R(0), 1.0, None, ALU.add).then_inc(S["dve_done"], 1)
                e.wait_ge(S["dve_done"], t_.due("dve_done"))
                v.reciprocal(R(0), R(0)).then_inc(S["dve_done"], 1)
                e.wait_ge(S["dve_done"], t_.due("dve_done"))
                v.tensor_tensor(R(1), R(0), cst("rbias").unsqueeze(1).to_broadcast([P, NT, NE]), ALU.add)\
                    .then_inc(S["dve_done"], 1)
                e.wait_ge(S["dve_done"], t_.due("dve_done"))
                m = G(1)
                v.tensor_tensor(pairs[:, :, 0:3], m[:, :, 0:1].to_broadcast([P, NT * NG, 3]), m[:, :, 1:4], ALU.add)
                v.tensor_tensor(pairs[:, :, 3:5], m[:, :, 1:2].to_broadcast([P, NT * NG, 2]), m[:, :, 2:4], ALU.add)
                v.tensor_tensor(pairs[:, :, 5:6], m[:, :, 2:3], m[:, :, 3:4], ALU.add).then_inc(S["dve_done"], 1)
                e.wait_ge(S["dve_done"], t_.due("dve_done"))
                v.tensor_reduce(few[:, 0, :], pairs[:, :, :], AX, ALU.max).then_inc(S["dve_done"], 1)
                e.wait_ge(S["dve_done"], t_.due("dve_done"))
                by = lambda k: few[:, k, :].rearrange("p (t g) -> p t g", t=NT)
                v.tensor_reduce(few[:, 1, 0:NT], by(0), AX, ALU.max).then_inc(S["dve_done"], 1)
                e.wait_ge(S["dve_done"], t_.due("dve_done"))
                v.tensor_tensor(by(2), by(0), over(few[:, 1, 0:NT], NG), ALU.is_ge).then_inc(S["dve_done"], 1)
                e.wait_ge(S["dve_done"], t_.due("dve_done"))
                v.tensor_tensor(few[:, 2, :], few[:, 2, :], cst("gcode"), ALU.mult).then_inc(S["dve_done"], 1)
                e.wait_ge(S["dve_done"], t_.due("dve_done"))
                v.tensor_reduce(few[:, 3, 0:NT], by(2), AX, ALU.max).then_inc(S["dve_done"], 1)
                e.wait_ge(S["dve_done"], t_.due("dve_done"))
                v.tensor_tensor(by(2), by(2), over(few[:, 3, 0:NT], NG), ALU.is_equal).then_inc(S["dve_done"], 1)
                e.wait_ge(S["dve_done"], t_.due("dve_done"))
                v.tensor_scalar(few[:, 2, :], few[:, 2, :], BIG, -BIG, ALU.mult, ALU.add).then_inc(S["dve_done"], 1)
                e.wait_ge(S["dve_done"], t_.due("dve_done"))
                v.tensor_tensor(G(2), G(1), over(few[:, 2, :], EG), ALU.add).then_inc(S["dve_done"], 1)
                e.wait_ge(S["dve_done"], t_.due("dve_done"))
                ecode = cst("ecode").rearrange("p (t n) -> p t n", t=NT)
                for k in (4, 5):
                    v.tensor_reduce(few[:, 4, 0:NT], R(2), AX, ALU.max).then_inc(S["dve_done"], 1)
                    e.wait_ge(S["dve_done"], t_.due("dve_done"))
                    v.tensor_tensor(R(3), R(2), over(few[:, 4, 0:NT], NE), ALU.is_ge).then_inc(S["dve_done"], 1)
                    e.wait_ge(S["dve_done"], t_.due("dve_done"))
                    v.tensor_tensor(R(3), R(3), ecode, ALU.mult).then_inc(S["dve_done"], 1)
                    e.wait_ge(S["dve_done"], t_.due("dve_done"))
                    v.tensor_reduce(few[:, 5, 0:NT], R(3), AX, ALU.max).then_inc(S["dve_done"], 1)
                    e.wait_ge(S["dve_done"], t_.due("dve_done"))
                    v.tensor_tensor(R(k), R(3), over(few[:, 5, 0:NT], NE), ALU.is_equal).then_inc(S["dve_done"], 1)
                    e.wait_ge(S["dve_done"], t_.due("dve_done"))
                    if k == 4:
                        v.scalar_tensor_tensor(out=R(2), in0=R(4), scalar=-2.0 * BIG, in1=R(2),
                                               op0=ALU.mult, op1=ALU.add).then_inc(S["dve_done"], 1)
                        e.wait_ge(S["dve_done"], t_.due("dve_done"))
                v.tensor_tensor(R(7), R(4), R(5), ALU.add).then_inc(S["mask_ready"], 1)
                e.wait_ge(S["mask_ready"], t_.due("mask_ready"))
                v.tensor_tensor(R(6), R(0), R(7), ALU.mult).then_inc(S["dve_done"], 1)
                e.wait_ge(S["dve_done"], t_.due("dve_done"))
                v.tensor_reduce(few[:, 4, 0:NT], R(6), AX, ALU.add).then_inc(S["dve_done"], 1)
                e.wait_ge(S["dve_done"], t_.due("dve_done"))
                v.reciprocal(few[:, 5, 0:NT], few[:, 4, 0:NT]).then_inc(S["dve_done"], 1)
                e.wait_ge(S["dve_done"], t_.due("dve_done"))
                token = over(cst("token"), NE)
                v.tensor_copy(info[:, :, :, 0], token)
                v.scalar_tensor_tensor(out=info[:, :, :, 1], in0=R(5), scalar=float(SEQ), in1=token,
                                       op0=ALU.mult, op1=ALU.add)
                v.tensor_copy(info[:, :, :, 3], token)
                v.tensor_tensor(info[:, :, :, 2], R(6), over(few[:, 5, 0:NT], NE), ALU.mult)\
                    .then_inc(S["dve_done"], 1)
                e.wait_ge(S["dve_done"], t_.due("dve_done"))
                e.wait_ge(S["rank_banked"], t_.due("rank_banked"))
                v.scalar_tensor_tensor(out=R(3),
                                       in0=bank[5][:, 0:NT * NE].rearrange("p (t n) -> p t n", t=NT),
                                       scalar=1.0, in1=R(7), op0=ALU.add, op1=ALU.mult).then_inc(S["dve_done"], 1)
                e.wait_ge(S["dve_done"], t_.due("dve_done"))
                v.tensor_copy(left[:, :], bank[5][:, NT * NE:(NT + 1) * NE])
                v.tensor_scalar(R(3), R(3), -1.0, None, ALU.add).then_inc(S["dve_done"], 1)
                e.wait_ge(S["dve_done"], t_.due("dve_done"))

                def rows_lo(b):
                    for g in range(4):
                        e.wait_ge(S["xt_hi"], t_.due("xt_hi"))
                        k, n = slice(4 * g, 4 * g + 4), slice(b * P, (b + 1) * P)
                        v.tensor_tensor(xl[:, k, n], bank[6 + g % 2][:, :].rearrange("p (c n) -> p c n", c=4),
                                        xh[:, k, n].bitcast(F32), ALU.subtract).then_inc(S["xt_lo"], 1)

                def expert(b, k):
                    for h in range(2 * EXP_UNITS):
                        cut(h)
                        if h == 11:
                            e.wait_ge(S["sig_exp"], t_.due("sig_exp"))
                            v.tensor_scalar(act_tmp, act_tmp, 1.0, None, ALU.add).then_inc(S["dve_done"], 1)
                            e.wait_ge(S["dve_done"], t_.due("dve_done"))
                            v.reciprocal(act_rec, act_tmp).then_inc(S["dve_done"], 1)
                            e.wait_ge(S["dve_done"], t_.due("dve_done"))
                            v.tensor_tensor(act_tmp, bank[0][:, :], act_rec, ALU.mult).then_inc(S["dve_done"], 1)
                            e.wait_ge(S["dve_done"], t_.due("dve_done"))
                            rows_lo(1 - b)
                        if h == 19:
                            v.scalar_tensor_tensor(out=act, in0=act_tmp, scalar=slots[:, bass.ds(k, 1), 2:3]
                                                   .rearrange("p a b -> p (a b)"), in1=bank[1][:, :],
                                                   op0=ALU.mult, op1=ALU.mult).then_inc(S["act_ready"], 1)
                            e.wait_ge(S["act_hi"], t_.due("act_hi"))
                            v.tensor_tensor(actTl[:, :, :], bank[6][:, :].rearrange("p (c n) -> p c n", c=4),
                                            actTh[:, :, :].bitcast(F32), ALU.subtract).then_inc(S["act_lo"], 1)

                with t_.one_round():
                    e.wait_ge(S["again_read"], t_.due("again_read", 4))
                    v.tensor_scalar(left[:, :], left[:, :], -float(SLOTS), None, ALU.add).then_inc(S["dve_done"], 1)
                    e.wait_ge(S["dve_done"], t_.due("dve_done"))
                    v.tensor_reduce(more[0:1, 0:1], left[0:1, :], AX, ALU.max).then_inc(S["dve_done"], 1)
                    e.wait_ge(S["dve_done"], t_.due("dve_done"))
                    v.tensor_scalar(again[0:1, 0:1], more[0:1, 0:1], 0.0, None, ALU.is_gt)\
                        .then_inc(S["again_ready"], 1)
                    for k in range(NE):
                        if k >= 2:
                            e.wait_ge(S["slot_banked"], t_.due("slot_banked"))
                        for t in range(NT):
                            last = v.tensor_scalar(chosen[:, k % 2, t, :], cst("slot"), route[:, 3, t, k:k + 1],
                                                   None, ALU.is_equal)
                        last.then_inc(S["chosen_ready"], 1)
                    e.wait_ge(S["slot_banked"], t_.due("slot_banked", 2))
                    v.tensor_copy(slots[:, :, :], bank[6][:, 0:4 * NE].rearrange("p (n k) -> p n k", k=4))\
                        .then_inc(S["dve_done"], 1)
                    e.wait_ge(S["dve_done"], t_.due("dve_done"))
                    v.tensor_scalar(pick[:, 0, :], slots[:, :, 0], 0.0, NOWHERE, ALU.is_equal, ALU.mult)\
                        .then_inc(S["dve_done"], 1)
                    e.wait_ge(S["dve_done"], t_.due("dve_done"))
                    for k, at in ((0, tok_at), (1, put_at)):
                        v.scalar_tensor_tensor(out=at[:, :, 0], in0=slots[:, :, k], scalar=-1.0,
                                               in1=pick[:, 0, :], op0=ALU.add, op1=ALU.add)
                    v.tensor_scalar(R(3), R(3), -float(SLOTS), None, ALU.add).then_inc(S["tables_ready"], 1)
                    e.wait_ge(S["tables_ready"], t_.due("tables_ready"))
                    rows_lo(0)
                    with t_.loop(e.Fori(0, NE // 2)) as i:
                        expert(0, i * 2)
                        expert(1, i * 2 + 1)

                e.wait_ge(S["picks_landed"], t_.due("picks_landed", 32 * NT))
                for k in range(2):
                    for t in range(NT):
                        ins = v.tensor_tensor(x[:, t, :], x[:, t, :], picked[k * NT + t], ALU.add)
                    ins.then_inc(S["dve_done"], 1)
                    e.wait_ge(S["dve_done"], t_.due("dve_done"))
                e.sem_inc(S["x_ready"], NT)


_INS = ("x", "in_units", "forget_w", "out_units", "expert_units", "norms", "small", "const", "router")


def kernel(x, attn_norm, w_in, b_forget, qnorm_diff, knorm_diff, lam_q1, lam_k1, lam_q2, lam_k2,
           subln_diff, onorm_sb, qnorm_fox, knorm_fox, onorm_fox, w_out, ffn_norm,
           w_router, router_bias, w_gate, w_up, w_down):
    import math

    import concourse.bacc as bacc
    from concourse.bass_utils import run_bass_kernel_spmd as run

    x, w_in, w_out, w_gate, w_up, w_down = (np.asarray(a) for a in (x, w_in, w_out, w_gate, w_up, w_down))
    w_router = np.asarray(w_router)

    def by_columns(w):
        lead, n = w.shape[:-2], w.shape[-1] // COLS
        w = w.reshape(-1, D // (4 * P), 4, P, n, COLS)
        return np.ascontiguousarray(w.transpose(0, 4, 1, 3, 2, 5)).reshape(*lead, n * (D // (4 * P)), P, UNIT)

    experts = np.concatenate([by_columns(w_gate), by_columns(w_up), w_down.reshape(DEPTH, NE, F // P, P, UNIT)], 2)
    forget = w_in[:, :, WIN:].reshape(DEPTH, NC, P, HC).transpose(0, 2, 1, 3)
    forget = np.concatenate([forget, np.zeros((DEPTH, P, NC, FPAD - HC), np.float32)], 3)
    small = np.zeros((DEPTH, P, SMALL), np.float32)

    def put(name, a):
        small[:, :, SM[name][0]:SM[name][1]] = a

    for name, a, times in (("gqa", qnorm_diff, 2), ("gka", knorm_diff, 2), ("gqc", qnorm_fox, 1),
                           ("gkc", knorm_fox, 1), ("goa", subln_diff, 1), ("gob", onorm_sb, 1),
                           ("goc", onorm_fox, 1)):
        put(name, np.tile(np.asarray(a), (1, times))[:, :, None])
    put("bf", np.asarray(b_forget)[:, None, :])
    put("lam", np.concatenate([np.asarray(a) for a in (lam_q1, lam_k1, lam_q2, lam_k2)], 1)[:, None, :])
    init = np.array([0.8 - 0.6 * math.exp(-0.3 * k) for k in range(DEPTH)])
    put("init", init[:, None, None])
    put("rest", (1.0 - init)[:, None, None])
    const = shape_constants()
    const[:, CN["rbias"][0]:CN["rbias"][1]] = np.asarray(router_bias)[None, :]
    arrays = dict(zip(_INS, (
        x.reshape(SEQ, D), by_columns(w_in[:, :, :WIN]).reshape(-1, P, UNIT), forget,
        by_columns(w_out).reshape(-1, P, UNIT), experts.reshape(-1, P, UNIT),
        np.stack([np.asarray(attn_norm), np.asarray(ffn_norm)], 1).reshape(2 * DEPTH, D), small, const,
        w_router.reshape(NC, P, NE).transpose(1, 0, 2))))
    arrays = {f"in_{k}": np.ascontiguousarray(a) for k, a in arrays.items()}

    nc = bacc.Bacc("TRN2", target_bir_lowering=False, num_devices=1)
    args = [nc.dram_tensor(k, a.shape, mybir.dt.from_np(a.dtype), kind="ExternalInput").ap()
            for k, a in arrays.items()]
    rows_dram = nc.dram_tensor("expert_rows", (SEQ, D), F32, kind="Internal").ap()
    picks_dram = nc.dram_tensor("picks", (2 * SEQ, D), F32, kind="Internal").ap()
    out = nc.dram_tensor("out_rows", (SEQ, D), F32, kind="ExternalOutput").ap()
    trunk(nc, *args, rows_dram, picks_dram, out)
    r = run(nc, [arrays], core_ids=[0])
    return r.results[0]["out_rows"].reshape(1, SEQ, D)
```

```python
from contextlib import ExitStack, contextmanager

import numpy as np

import concourse.bass as bass
from concourse import mybir

F32 = mybir.dt.float32
F32R = mybir.dt.float32r
I32 = mybir.dt.int32
U32 = mybir.dt.uint32
ALU = mybir.AluOpType
ACT = mybir.ActivationFunctionType
AX = mybir.AxisListType.X

P = 128
D, SEQ, DEPTH = 2048, 256, 2
NT = SEQ // P
NC = D // P
HD = 128
NH = D // HD
HB = HC = NH // 3
HA = NH - HB - HC
WIN = 3 * D
FPAD = HC + 1
NE, NG, F = 16, 4, D // 4
EG = NE // NG
EPS = 1e-6
SLOTS = P
BIG = 1e30
NOWHERE = 1048576.0

COLS = 512
UNIT = 4 * COLS
HALF = UNIT // 2
PART = 2 * D * F // (P * UNIT)
IN_UNITS = WIN * D // (P * UNIT)
OUT_UNITS = D * D // (P * UNIT)
EXP_UNITS = 3 * D * F // (P * UNIT)
NBLOCKS = (IN_UNITS + OUT_UNITS) // 4
RAW = 4
CUT = 4

QA, KA, VA = 0, HA * HD, 2 * HA * HD
QB, KB, VB = 3 * HA * HD, (3 * HA + HB) * HD, (3 * HA + 2 * HB) * HD
QC = 3 * (HA + HB) * HD
KC, VC = QC + HC * HD, QC + 2 * HC * HD
HEADS = [(g, i) for i in range(HA) for g in "abc" if i < {"a": HA, "b": HB, "c": HC}[g]]
QKV = {"a": (QA, KA, VA), "b": (QB, KB, VB), "c": (QC, KC, VC)}
MIX = {"a": 0, "b": HA, "c": HA + HB}
HALVES_A = 4 * HA
NORMS = HALVES_A + 2 * HC
SPAN = P + SEQ
ROWS = (slice(0, P), slice(P, SPAN))

SM = {}
_at = 0
for _name, _n in (("gqa", 1), ("gka", 1), ("gqc", 1), ("gkc", 1), ("goa", 1), ("gob", 1), ("goc", 1),
                  ("bf", HC), ("lam", 4 * 64), ("init", 1), ("rest", 1)):
    SM[_name] = (_at, _at + _n)
    _at += _n
SMALL = _at
CN = {}
_at = 0
for _name, _n in (("ident", P), ("before", P), ("ones", P), ("before2", P), ("upto", P), ("after", P),
                  ("ndist", SPAN), ("causal", P), ("slot", P), ("token", NT), ("gcode", NT * NG),
                  ("ecode", NT * NE), ("rbias", NE)):
    CN[_name] = (_at, _at + _n)
    _at += _n
CONST = _at


TURN = {False: {PART + 1: 0, PART + 3: 1, PART + 5: 2, PART + 7: 3}, True: {1: 0, 3: 1, 5: 2, 7: 3}}
TURNED = {f: {h + CUT + 1: g for h, g in at.items()} for f, at in TURN.items()}
SILU = PART + CUT - 1
GATED = CUT - 1
ACT_TURN = GATED + 1
STORE = {2 * PART + CUT - 1: 0, 2 * PART + CUT + 1: 1, 2 * PART + CUT + 2: 2, 2 * PART + CUT + 3: 3}


def shape_constants():
    t = np.zeros((P, CONST), np.float32)
    i, j = np.arange(P)[:, None], np.arange(P)[None, :]

    def put(name, v):
        t[:, CN[name][0]:CN[name][1]] = v

    put("ident", i == j)
    put("before", i < j)
    put("before2", i < j)
    put("ones", 1.0)
    put("upto", i <= j)
    put("after", i > j)
    q = np.concatenate([np.broadcast_to(i, (P, P)), np.broadcast_to(i + P, (P, SEQ))], 1)
    k = np.concatenate([np.arange(P), np.arange(SEQ)])[None, :]
    put("ndist", np.where(k // 64 <= q // 64, -np.abs(q - k), -BIG))
    put("causal", np.where(j <= i, 0.0, -BIG))
    put("slot", j)
    put("token", np.arange(P)[:, None] + P * np.arange(NT)[None, :] + 1)
    put("gcode", np.tile(NG - np.arange(NG), NT)[None, :])
    put("ecode", np.tile(NE - np.arange(NE), NT)[None, :])
    return t


FIXED = {
    "gain_landed": (32, 0), "small_landed": (32, 0), "rows_stored": (16 * NT, 0),
    "picks_landed0": (16 * NT, 0), "picks_landed1": (16 * NT, 0),
    "x_ready": (2 * NT, 0), "rows_squared": (2, 0), "log_ready": (4, 0), "root_ready": (4, 0),
    "rows_ready": (2 * NT, 0), "gain_free": (1, 0), "t_banked": (3 * NC // 2, 0), "t_hi": (3 * NC // 2, 0),
    "t_lo": (3 * NC // 2, 0), "f_hi": (1, 0), "f_lo": (1, 0), "f_banked": (1, 0), "f_ready": (1, 0),
    "f_log": (1, 0), "logf_ready": (1, 0), "lam_dots": (1, 0), "lam_exp": (1, 0), "d_banked": (1, 0),
    "d_ready": (1, 0), "sums_written": (IN_UNITS // 4, 0), "d_turned": (1, 0), "dT_ready": (1, 0),
    "head_norms": (1, 0), "q_banked": (NH, 0), "k_banked": (NH, 0), "qT_ready": (NH, 0),
    "kT_ready": (NH, 0), "s_banked": (NH, 0), "z_ready": (HB, 0), 
    "soft_ready": (HB, 0), "keep_ready": (HB, 0), "sum_ready": (HB, 0), "a_ready": (HB, 0),
    "aT_ready": (HB, 0), "neg_max": (HA + HC, 0), "exps_ready": (HA + HC, 0), "weights_ready": (HA, 0),
    "sums_ready": (HC, 0), "m_banked": (NH, 0), "wT_ready": (HA + HC, 0), "o_banked": (NH, 0),
    "o_ready": (NH, 0), "mix_scaled": (NT, 0), "r_banked": (1, 0), "r_summed": (1, 0),
    "r_exp": (1, 0), "mask_ready": (1, 0),
    "rank_banked": (1, 0), "block_out": (NBLOCKS, 0), "cut_free": (2 * (IN_UNITS + OUT_UNITS), 2 * NE * EXP_UNITS),
    "again_ready": (0, 1), "again_read": (0, 4), "chosen_ready": (0, NE), "slot_banked": (0, NE),
    "tables_ready": (0, 1),
}


class Tally:

    def __init__(self, e, sems, start=None, counted=()):
        self.e, self.sems = e, sems
        self.start = start or {}
        self.layer = 0
        self.rounds = e.alloc_register("rounds")
        e.reg_mov(self.rounds, 0)
        self.reg, self.base, self.n, self.in_round = {}, {}, {}, False
        for k in counted:
            self.reg[k] = e.alloc_register(f"seen_{k}")
            e.reg_mov(self.reg[k], self.start.get(k, 0))

    def due(self, k, n=1):
        e = self.e
        self.n[k] = self.n.get(k, 0) + n
        if k in self.reg:
            if k not in self.base:
                self.base[k] = e.snap(self.reg[k])
            value = self.base[k] + self.n[k]
        else:
            a, b = FIXED[k]
            value = self.start.get(k, 0) + self.n[k] + self.layer * a
            if b:
                if "rounds" not in self.base:
                    self.base["rounds"] = e.snap(self.rounds)
                value = value + self.base["rounds"] * b
        return value

    def fence(self):
        self.e.sem_inc(self.sems["fence"], 1)

    def by(self, k, n):
        return self.due(k, n - self.n.get(k, 0))

    def ahead(self, k, n):
        value = self.due(k, n)
        self.n[k] -= n
        return value

    def settle(self):
        for k, r in self.reg.items():
            if self.n.get(k):
                self.e.reg_add(r, r, self.n[k])
                self.n[k] = 0
        self.base.clear()

    @contextmanager
    def loop(self, cm):
        self.fence()
        self.settle()
        fixed = {k: n for k, n in self.n.items() if k not in self.reg}
        with cm as i:
            self.base.clear()
            yield i
            self.settle()
            now = {k: n for k, n in self.n.items() if k not in self.reg}
            assert all(n == fixed.get(k, 0) for k, n in now.items()), (fixed, now)

    @contextmanager
    def layers(self):
        with self.loop(self.e.Fori(0, DEPTH)) as layer:
            self.layer = layer
            yield layer
            self.layer = 0
            for k, n in self.n.items():
                if k not in self.reg:
                    assert n <= FIXED[k][0], (k, n)
                    self.n[k] = 0

    @contextmanager
    def one_round(self):
        e = self.e
        go = e.alloc_register("go")
        self.fence()
        e.reg_mov(go, 1)
        self.settle()
        with self.loop(e.While(lambda: e.snap(go))):
            before = dict(self.n)
            yield
            e.wait_ge(self.sems["again_ready"], self.due("again_ready"))
            self.fence()
            e.reg_mov(go, e.value_load(self.again, min_val=0, max_val=1))
            if self.tells:
                e.sem_inc(self.sems["again_read"], 1)
            for k in self.n:
                if k not in self.reg:
                    assert self.n[k] - before.get(k, 0) in (0, FIXED[k][1]), (k, self.n[k])
                    self.n[k] = before.get(k, 0)
            e.reg_add(self.rounds, self.rounds, 1)


def trunk(nc, x_in, in_units, forget_w, out_units, expert_units, norms, small_in, const_in, router_in,
          rows_dram, picks_dram, out):
    with ExitStack() as ctx:
        def sb(name, shape, dt=F32):
            return ctx.enter_context(nc.sbuf_tensor(name, shape, dt))

        def sem(name):
            return ctx.enter_context(nc.semaphore(name))

        bank = [ctx.enter_context(nc.psum_tensor(f"bank{i}", [P, COLS], F32)) for i in range(8)]

        x = sb("x", [P, NT, D])
        xh = sb("xh", [P, NC, SEQ], F32R)
        xl = sb("xl", [P, NC, SEQ], F32R)
        proj = sb("proj", [P, NT, WIN])
        rows = sb("rows", [P, NT, D])
        wide = sb("wide", [P, D])
        raw = sb("raw", [P, RAW, UNIT])
        wh = sb("wh", [P, CUT, HALF], F32R)
        wl = sb("wl", [P, CUT, HALF], F32R)
        const = sb("const", [P, CONST])
        small = sb("small", [P, SMALL])
        qkT = sb("qkT", [P, 2, 2, SEQ])
        wT = sb("wT", [P, 2, SPAN])
        actTh = sb("actTh", [P, F // P, SLOTS], F32R)
        actTl = sb("actTl", [P, F // P, SLOTS], F32R)
        fc = sb("fc", [P, NC, 2 * FPAD], F32R)
        fcr = sb("fcr", [P, NC, FPAD])
        rt = sb("rt", [P, NC, 2 * NE], F32R)
        stat = sb("stat", [P, 3, NT, NORMS])
        soft = sb("soft", [P, 3, 4, 4])
        logf = sb("logf", [P, 3, NT, HC])
        dcum = sb("dcum", [P, NT, HC])
        ndcT = sb("ndcT", [HC, SEQ])
        lam = sb("lam", [P, 4])
        more = sb("more", [1, 2])
        again = sb("again", [1, 1], I32)
        tok_at = sb("tok_at", [P, NE, 1], U32)
        put_at = sb("put_at", [P, NE, 1], U32)

        turned_qk = qkT[:, :, :, :].rearrange("p a b n -> p (a b n)")

        def table(at, width, form=None, **sizes):
            ap = turned_qk[:, at:at + width]
            return ap.rearrange(form, **sizes) if form else ap

        route = table(0, 8 * NT * NE, "p (k t n) -> p k t n", k=8, t=NT)
        pairs = table(256, 6 * NT * NG, "p (g n) -> p g n", n=6)
        few = table(304, 6 * NT * NG, "p (k g) -> p k g", k=6)
        info = table(352, 4 * NT * NE, "p (t n k) -> p t n k", t=NT, k=4)
        slots = table(480, 4 * NE, "p (n k) -> p n k", k=4)
        pick = table(544, 2 * NE, "p (k n) -> p k n", k=2)
        left = table(576, NE)

        sums = table(0, NT * WIN // 64, "p (t n) -> p t n", t=NT)

        def cst(name):
            return const[:, CN[name][0]:CN[name][1]]

        def sml(name):
            return small[:, SM[name][0]:SM[name][1]]

        ident, after, upto = cst("ident"), cst("after"), cst("upto")
        before, ones = cst("before"), cst("ones")
        strict = const[:, CN["before"][0]:CN["before2"][1]]
        score = wide[:, 0:4 * SPAN].rearrange("p (a b n) -> p a b n", a=2, b=2)
        chosen = wide[:, 0:4 * P].rearrange("p (a t n) -> p a t n", a=2, t=NT)
        router_raw = rows[:, 0, 0:NC * NE].rearrange("p (c n) -> p c n", c=NC)

        spare = proj[:, :, :].rearrange("p t n -> p (t n)")
        gathered = [spare[:, b * D:(b + 1) * D] for b in range(2)]
        expert_out = [spare[:, (2 + b) * D:(3 + b) * D] for b in range(2)]
        picked = gathered + expert_out
        act_tmp = spare[:, 4 * D:4 * D + F]
        act_rec = spare[:, 4 * D + F:4 * D + 2 * F]
        act = spare[:, 4 * D + 2 * F:4 * D + 3 * F]

        S = {n: sem(n) for n in (
            "start_landed x_landed out_stored router_ready hi_ready lo_ready cut_free block_out "
            "xt_banked xt_hi xt_lo sig_exp act_ready act_banked act_hi act_lo sq_ready silu_ready out_ready out_free "
            "act_done dve_done fence").split() + [k for k in FIXED if k not in ("cut_free", "block_out")]}
        for i in range(RAW):
            S[f"raw_landed{i}"] = sem(f"raw_landed{i}")
        for i in range(2):
            S[f"gather_landed{i}"] = sem(f"gather_landed{i}")
            S[f"scattered{i}"] = sem(f"scattered{i}")

        def tally(e, start=None, counted=(), tells=True):
            t = Tally(e, S, start, counted)
            t.again, t.tells = again[0:1, 0:1], tells
            return t

        block = ctx.enter_context(nc.Block())

        @block.sync
        def _(e):
            e.dma_start(const[:, :], const_in).then_inc(S["start_landed"], 16)
            e.dma_start(router_raw, router_in).then_inc(S["start_landed"], 16)
            for t in range(NT):
                e.dma_start(x[:, t, :], x_in[t * P:(t + 1) * P, :]).then_inc(S["x_landed"], 16)
            t_ = tally(e, counted=("lo_ready",))

            def load(units, at):
                for j in range(RAW):
                    e.wait_ge(S["lo_ready"], t_.due("lo_ready", 2))
                    e.dma_start(raw[:, j, :], units[bass.ds(at + j, 1)].rearrange("o p n -> (o p) n"))\
                        .then_inc(S[f"raw_landed{j}"], 16)

            with t_.layers() as layer:
                with t_.loop(e.Fori(0, IN_UNITS // RAW)) as i:
                    load(in_units, layer * IN_UNITS + i * RAW)
                with t_.loop(e.Fori(0, OUT_UNITS // RAW)) as i:
                    load(out_units, layer * OUT_UNITS + i * RAW)
                with t_.one_round():
                    with t_.loop(e.Fori(0, NE * EXP_UNITS // RAW)) as i:
                        load(expert_units, layer * (NE * EXP_UNITS) + i * RAW)
            e.wait_ge(S["x_ready"], NT * (2 * DEPTH + 1))
            for t in range(NT):
                e.dma_start(out[t * P:(t + 1) * P, :], x[:, t, :]).then_inc(S["out_stored"], 16)
            e.wait_ge(S["out_stored"], 16 * NT)

        @block.gpsimd
        def _(e):
            t_ = tally(e, start={"out_ready": 1},
                       counted=("xt_banked", "out_ready", "scattered0", "scattered1"))
            with t_.layers() as layer:
                e.dma_start(small[:, :], small_in[bass.ds(layer, 1)].rearrange("o p n -> (o p) n"))\
                    .then_inc(S["small_landed"], 16)
                e.dma_start(fcr[:, :, :], forget_w[bass.ds(layer, 1)].rearrange("o p c n -> (o p) c n"))\
                    .then_inc(S["small_landed"], 16)
                for k in range(2):
                    if k == 1:
                        e.wait_ge(S["gain_free"], t_.due("gain_free"))
                        t_.fence()
                    e.dma_start(wide[:, :], norms[bass.ds(layer * 2 + k, 1)].to_broadcast([P, D]))\
                        .then_inc(S["gain_landed"], 16)
                    e.wait_ge(S["rows_ready"], t_.due("rows_ready", NT))
                    t_.fence()
                for t in range(NT):
                    e.dma_start(rows_dram[t * P:(t + 1) * P, :], rows[:, t, :]).then_inc(S["rows_stored"], 16)
                e.wait_ge(S["rows_stored"], t_.due("rows_stored", 16 * NT))
                t_.fence()

                def gather(k):
                    e.indirect_dma_start(gathered[k % 2], None, rows_dram[:, :],
                                         bass.IndirectOffsetOnAxis(ap=tok_at[:, k % NE, :], axis=0),
                                         bounds_check=SEQ - 1, oob_is_err=False)\
                        .then_inc(S[f"gather_landed{k % 2}"], 16)

                def scatter(k):
                    e.wait_ge(S["out_ready"], t_.due("out_ready"))
                    t_.fence()
                    e.indirect_dma_start(picks_dram[:, :],
                                         bass.IndirectOffsetOnAxis(ap=put_at[:, k, :], axis=0),
                                         expert_out[k % 2], None,
                                         bounds_check=2 * SEQ - 1, oob_is_err=False)\
                        .then_inc(S[f"scattered{k % 2}"], 16)

                def freed(k):
                    e.wait_ge(S[f"scattered{k % 2}"], t_.due(f"scattered{k % 2}", 16))
                    t_.fence()
                    e.sem_inc(S["out_free"], 1)

                with t_.one_round():
                    e.wait_ge(S["tables_ready"], t_.due("tables_ready"))
                    t_.fence()
                    gather(0)
                    gather(1)
                    for k in range(NE + 2):
                        if k < NE:
                            e.wait_ge(S["xt_banked"], t_.due("xt_banked", 4))
                            t_.fence()
                        if k + 2 < NE:
                            gather(k + 2)
                        if k >= 3:
                            freed(k - 3)
                        if k >= 2:
                            scatter(k - 2)
                    freed(NE - 1)
                for k in range(2 * NT):
                    e.dma_start(picked[k], picks_dram[k * P:(k + 1) * P, :])\
                        .then_inc(S[f"picks_landed{k // NT}"], 16)

        @block.scalar
        def _(e):
            act_ = nc.scalar.activation
            t_ = tally(e, start={"block_out": 2}, counted=(
                "cut_free", "block_out", "raw_landed0", "raw_landed1", "raw_landed2", "raw_landed3",
                "xt_banked", "act_banked", "out_free", "act_done"))

            def cut(h):
                if h % 2 == 0:
                    e.wait_ge(S[f"raw_landed{h // 2 % RAW}"], t_.due(f"raw_landed{h // 2 % RAW}", 16))
                e.wait_ge(S["cut_free"], t_.due("cut_free"))
                act_(wh[:, h % CUT, :], raw[:, h // 2 % RAW, h % 2 * HALF:(h % 2 + 1) * HALF], ACT.Copy)\
                    .then_inc(S["hi_ready"], 1)

            def root(n):
                e.wait_ge(S["log_ready"], t_.due("log_ready"))
                act_(stat[:, 1, :, 0:n], stat[:, 0, :, 0:n], ACT.Ln).then_inc(S["act_done"], 1)
                e.wait_ge(S["act_done"], t_.due("act_done"))
                act_(stat[:, 1, :, 0:n], stat[:, 1, :, 0:n], ACT.Exp, scale=-0.5).then_inc(S["root_ready"], 1)

            def norm_rows():
                act_(rows[:, 0, :], x[:, 0, :], ACT.Square, accum_out=stat[:, 0, 0, 0:1])\
                    .then_inc(S["rows_squared"], 1)
                root(1)
                for g in range(NC // 2):
                    e.wait_ge(S["t_banked"], t_.due("t_banked"))
                    act_(xh[:, 2 * g:2 * g + 2, :], bank[4 + g % 4][:, :].rearrange("p (c n) -> p c n", c=2),
                         ACT.Copy).then_inc(S["t_hi"], 1)

            e.wait_ge(S["start_landed"], 32)
            act_(rt[:, :, 0:NE], router_raw, ACT.Copy).then_inc(S["router_ready"], 1)
            e.wait_ge(S["router_ready"], 2)
            e.wait_ge(S["x_landed"], 16 * NT)

            with t_.layers():
                e.wait_ge(S["x_ready"], t_.due("x_ready", NT))
                norm_rows()
                e.wait_ge(S["small_landed"], t_.due("small_landed", 32))
                act_(fc[:, :, 0:FPAD], fcr[:, :, :], ACT.Copy).then_inc(S["f_hi"], 1)
                e.wait_ge(S["lam_dots"], t_.due("lam_dots"))
                act_(lam[:, 0:2], lam[:, 0:2], ACT.Exp).then_inc(S["lam_exp"], 1)
                def block_cut(behind=None):
                    for h in range(2 * RAW):
                        cut(h)
                        if h == 5 and behind is not None:
                            squares(*behind)

                def squares(j, b):
                    e.wait_ge(S["block_out"], t_.due("block_out"))
                    t_.fence()
                    for t in range(NT):
                        last = act_(rows[:, t, b * COLS:(b + 1) * COLS], proj[:, t, bass.ds(j * COLS, COLS)],
                                    ACT.Square)
                    last.then_inc(S["sq_ready"], 1)

                block_cut()
                with t_.loop(e.Fori(0, IN_UNITS // RAW // 2 - 1)) as i:
                    block_cut((i * 2, 0))
                    block_cut((i * 2 + 1, 1))
                block_cut((IN_UNITS // RAW - 2, 0))
                squares(IN_UNITS // RAW - 1, 1)
                root(NORMS)
                e.wait_ge(S["f_ready"], t_.due("f_ready"))
                act_(logf[:, 1, :, :], logf[:, 1, :, :], ACT.Exp).then_inc(S["act_done"], 1)
                e.wait_ge(S["act_done"], t_.due("act_done"))
                act_(logf[:, 1, :, :], logf[:, 1, :, :], ACT.Ln, bias=1.0).then_inc(S["f_log"], 1)


                e.wait_ge(S["d_banked"], t_.due("d_banked"))
                act_(dcum[:, :, :], bank[6][:, 0:NT * HC].rearrange("p (t h) -> p t h", t=NT), ACT.Copy)\
                    .then_inc(S["d_ready"], 1)
                e.wait_ge(S["d_turned"], t_.due("d_turned"))
                act_(ndcT[:, :], bank[6][0:HC, 0:SEQ], ACT.Copy, scale=-1.0).then_inc(S["dT_ready"], 1)

                def query(i):
                    g, _ = HEADS[i]
                    e.wait_ge(S["q_banked"], t_.by("q_banked", i + 1))
                    scale = {"a": sml("gqa"), "b": float(HD) ** -0.5, "c": sml("gqc")}[g]
                    act_(qkT[:, i % 2, 0, :], bank[4][:, 0:SEQ], ACT.Copy, scale=scale)\
                        .then_inc(S["qT_ready"], 1)

                def scores(i):
                    g, _ = HEADS[i]
                    b = i % 2
                    if g == "b":
                        e.wait_ge(S["s_banked"], t_.by("s_banked", i + 1))
                        if i >= 2:
                            e.wait_ge(S["m_banked"], t_.by("m_banked", i - 1))
                        act_(score[:, b, 0, :], bank[2 * b][:, 0:SPAN], ACT.Copy).then_inc(S["z_ready"], 1)
                        act_(score[:, b, 1, :], bank[2 * b][:, 0:SPAN], ACT.Abs).then_inc(S["act_done"], 1)
                        e.wait_ge(S["act_done"], t_.due("act_done"))
                        act_(score[:, b, 1, :], score[:, b, 1, :], ACT.Exp, scale=-1.0)\
                            .then_inc(S["act_done"], 1)
                        e.wait_ge(S["act_done"], t_.due("act_done"))
                        act_(score[:, b, 1, :], score[:, b, 1, :], ACT.Ln, bias=1.0)\
                            .then_inc(S["soft_ready"], 1)
                        return
                    e.wait_ge(S["neg_max"], t_.due("neg_max"))
                    for k in range(2 if g == "a" else 1):
                        for t, r in enumerate(ROWS):
                            c = 2 * t + k
                            last = act_(score[:, b, k, r], score[:, b, k, r], ACT.Exp,
                                        bias=soft[:, i % 3, 1, c:c + 1],
                                        accum_out=soft[:, i % 3, 2, c:c + 1])
                    last.then_inc(S["exps_ready"], 1)

                def turned(i):
                    g, _ = HEADS[i]
                    b = i % 2
                    if g == "b":
                        e.wait_ge(S["sum_ready"], t_.due("sum_ready"))
                        act_(score[:, b, 1, :], score[:, b, 1, :], ACT.Exp).then_inc(S["a_ready"], 1)
                        return
                    e.wait_ge(S["m_banked"], t_.by("m_banked", i + 1))
                    act_(wT[:, b, :], bank[6][:, 0:SPAN], ACT.Copy).then_inc(S["wT_ready"], 1)

                def output(i):
                    g, h = HEADS[i]
                    e.wait_ge(S["o_banked"], t_.by("o_banked", i + 1))
                    if g == "c":
                        e.wait_ge(S["sums_ready"], t_.due("sums_ready"))
                    at = (MIX[g] + h) * HD
                    for t in range(NT):
                        scale = soft[:, i % 3, 3, 2 * t:2 * t + 1] if g == "c" else 1.0
                        last = act_(rows[:, t, at:at + HD], bank[7][:, t * HD:(t + 1) * HD], ACT.Copy,
                                    scale=scale)
                    last.then_inc(S["o_ready"], 1)

                query(0)
                for i in range(NH + 2):
                    if i + 1 < NH:
                        query(i + 1)
                    if i < NH:
                        scores(i)
                    if i >= 2:
                        output(i - 2)
                    if 1 <= i <= NH:
                        turned(i - 1)

                e.wait_ge(S["o_ready"], t_.due("o_ready", NH))
                for t in range(NT):
                    act_(proj[:, t, 0:D], rows[:, t, :], ACT.Square).then_inc(S["sq_ready"], 1)
                root(NH)
                for g in range(NC // 2):
                    e.wait_ge(S["t_banked"], t_.due("t_banked"))
                    for c in (2 * g, 2 * g + 1):
                        gain = sml("goa" if c < HA else "gob" if c < HA + HB else "goc")
                        last = act_(xh[:, c, :], bank[4 + g % 4][:, c % 2 * SEQ:(c % 2 + 1) * SEQ], ACT.Copy,
                                    scale=gain)
                    last.then_inc(S["t_hi"], 1)

                with t_.loop(e.Fori(0, OUT_UNITS // RAW)):
                    for h in range(2 * RAW):
                        cut(h)
                e.wait_ge(S["block_out"], t_.due("block_out", OUT_UNITS // RAW))

                e.wait_ge(S["x_ready"], t_.due("x_ready", NT))
                norm_rows()
                e.wait_ge(S["r_summed"], t_.due("r_summed"))
                act_(route[:, 0, :, :], route[:, 0, :, :], ACT.Exp, scale=-1.0).then_inc(S["r_exp"], 1)

                def rows_hi(b, g):
                    e.wait_ge(S["xt_banked"], t_.due("xt_banked"))
                    act_(xh[:, 4 * g:4 * g + 4, b * P:(b + 1) * P],
                         bank[6 + g % 2][:, :].rearrange("p (c n) -> p c n", c=4), ACT.Copy)\
                        .then_inc(S["xt_hi"], 1)

                def act_hi():
                    e.wait_ge(S["act_banked"], t_.due("act_banked"))
                    act_(actTh[:, :, :], bank[6][:, :].rearrange("p (c n) -> p c n", c=4), ACT.Copy)\
                        .then_inc(S["act_hi"], 1)

                def store(b, k):
                    if k == 0:
                        e.wait_ge(S["out_free"], t_.due("out_free"))
                    ins = act_(expert_out[b][:, k * COLS:(k + 1) * COLS], bank[2 + k][:, :], ACT.Copy)
                    if k == 3:
                        ins.then_inc(S["out_ready"], 1)

                def step(b, first=False, last=False):
                    for h in range((2 if first else 3) * PART):
                        cut(h)
                        if h == PART and not first:
                            act_hi()
                        if h == SILU:
                            act_(act_tmp, bank[0][:, :], ACT.Exp, scale=-1.0).then_inc(S["sig_exp"], 1)
                        if h in TURNED[first] and not last:
                            rows_hi(1 - b, TURNED[first][h])
                        if h in STORE and not first:
                            store(1 - b, STORE[h])

                with t_.one_round():
                    for g in range(4):
                        rows_hi(0, g)
                    step(0, first=True)
                    with t_.loop(e.Fori(0, NE // 2 - 1)):
                        step(1)
                        step(0)
                    step(1, last=True)
                    for h in range(PART):
                        cut(h)
                        if h == GATED:
                            act_hi()
                    e.wait_ge(S["cut_free"], t_.ahead("cut_free", CUT))
                    for k in range(4):
                        store(1, k)

        @block.tensor
        def _(e):
            mm = nc.tensor.matmul
            t_ = tally(e, start={"lo_ready": 2 * RAW},
                       counted=("lo_ready", "block_out", "xt_lo", "act_ready", "act_lo", "out_ready", "silu_ready",
                                "gather_landed0", "gather_landed1"))

            def three(out, at, tok, rh, rl, start, stop):
                mm(out, xh[:, at, tok], rh, start=start, stop=False)
                mm(out, xh[:, at, tok], rl, start=False, stop=False)
                return mm(out, xl[:, at, tok], rh, start=False, stop=stop)

            def turn_rows(product=None):
                for g in range(NC // 2):
                    if g >= 4:
                        e.wait_ge(S["t_lo"], t_.due("t_lo"))
                    for c in range(2):
                        for t in range(NT):
                            at = (2 * c + t) * P
                            last = e.transpose(bank[4 + g % 4][:, at:at + P],
                                               rows[:, t, (2 * g + c) * P:(2 * g + c + 1) * P], ident)
                    last.then_inc(S["t_banked"], 1)
                    if product and g >= 4:
                        product(g - 4)
                for g in range(4, NC // 2):
                    e.wait_ge(S["t_lo"], t_.due("t_lo"))
                    if product:
                        last = product(g)
                return last

            def few_columns(first, n, w, chunks):
                for c in chunks:
                    for t in range(NT):
                        o = bank[first + t][:, 0:2 * n]
                        for k in (0, 1) if c < NC - 1 else (1, 0):
                            if k == 0:
                                last = mm(o, xh[:, c, t * P:(t + 1) * P], w[:, c, :], start=(c == 0),
                                          stop=(c == NC - 1))
                            else:
                                mm(o[:, 0:n], xl[:, c, t * P:(t + 1) * P], w[:, c, 0:n], start=False, stop=False)
                return last

            def blocks():
                for b in range(2):
                    e.wait_ge(S["block_out"], t_.due("block_out"))
                    for h in range(2 * RAW):
                        e.wait_ge(S["lo_ready"], t_.due("lo_ready"))
                        for c in range(2):
                            k = slice(c * COLS, (c + 1) * COLS)
                            for t in range(NT):
                                last = three(bank[2 * b + t][:, :], 2 * h + c, slice(t * P, (t + 1) * P),
                                             wh[:, h % CUT, k], wl[:, h % CUT, k],
                                             h + c == 0, h == 2 * RAW - 1 and c == 1)
                        last.then_inc(S["cut_free"], 1)

            def turn(i):
                g, h = HEADS[i]
                for k, done in enumerate(("q_banked", "k_banked")):
                    at = QKV[g][k] + h * HD
                    for t in range(NT):
                        last = e.transpose(bank[4 + k][:, t * P:(t + 1) * P], proj[:, t, at:at + HD], ident)
                    last.then_inc(S[done], 1)

            def scores(i):
                g, h = HEADS[i]
                b = i % 2
                qT, kT = qkT[:, b, 0, :], qkT[:, b, 1, :]
                e.wait_ge(S["qT_ready"], t_.due("qT_ready"))
                e.wait_ge(S["kT_ready"], t_.due("kT_ready"))
                if g == "a":
                    for k in range(2):
                        half = slice(64 * k, 64 * k + 64)
                        for t, r in enumerate(ROWS):
                            last = mm(bank[2 * b + k][:, r], qT[half, t * P:(t + 1) * P],
                                      kT[half, 0:(t + 1) * P], start=True, stop=True)
                elif g == "b":
                    mm(bank[2 * b][:, 0:SEQ], kT[:, 0:P], qT[:, :], start=True, stop=True)
                    last = mm(bank[2 * b][:, SEQ:SPAN], kT[:, P:SEQ], qT[:, P:SEQ], start=True, stop=True)
                else:
                    for t, r in enumerate(ROWS):
                        mm(bank[2 * b][:, r], qT[:, t * P:(t + 1) * P], kT[:, 0:(t + 1) * P],
                           start=True, stop=False)
                        last = mm(bank[2 * b][:, r], ident[0:HC, h:h + 1].to_broadcast([HC, P]),
                                  ndcT[:, 0:(t + 1) * P], start=False, stop=True)
                last.then_inc(S["s_banked"], 1)

            def middle(i):
                g, _ = HEADS[i]
                b = i % 2
                if g == "b":
                    keep = score[:, b, 0, :]
                    e.wait_ge(S["keep_ready"], t_.due("keep_ready"))
                    mm(bank[6][:, 0:P], after, keep[:, 0:P], start=True, stop=True)
                    mm(bank[6][:, P:SEQ], after, keep[:, P:SEQ], start=True, stop=False)
                    mm(bank[6][:, P:SEQ], ones, keep[:, SEQ:SPAN], start=False, stop=True)
                    last = mm(bank[6][:, SEQ:SPAN], after, keep[:, SEQ:SPAN], start=True, stop=True)
                else:
                    e.wait_ge(S["exps_ready"], t_.due("exps_ready"))
                    if g == "a":
                        e.wait_ge(S["weights_ready"], t_.due("weights_ready"))
                    for k in range(3):
                        last = e.transpose(bank[6][:, k * P:(k + 1) * P], score[:, b, 0, k * P:(k + 1) * P],
                                           ident)
                last.then_inc(S["m_banked"], 1)

            def output(i):
                g, h = HEADS[i]
                b = i % 2
                at = QKV[g][2] + h * HD
                if g == "b":
                    e.wait_ge(S["aT_ready"], t_.due("aT_ready"))
                else:
                    e.wait_ge(S["wT_ready"], t_.due("wT_ready"))
                if i:
                    e.wait_ge(S["o_ready"], t_.due("o_ready"))
                mm(bank[7][:, 0:HD], wT[:, b, 0:P], proj[:, 0, at:at + HD], start=True, stop=True)
                for u in range(NT):
                    last = mm(bank[7][:, HD:2 * HD], wT[:, b, (1 + u) * P:(2 + u) * P],
                              proj[:, u, at:at + HD], start=(u == 0), stop=(u == 1))
                last.then_inc(S["o_banked"], 1)

            def turn_gathered(b, g):
                if g == 0:
                    e.wait_ge(S[f"gather_landed{b}"], t_.due(f"gather_landed{b}", 16))
                if g >= 2:
                    e.wait_ge(S["xt_lo"], t_.due("xt_lo"))
                for c in range(4):
                    at = (4 * g + c) * P
                    last = e.transpose(bank[6 + g % 2][:, c * P:(c + 1) * P], gathered[b][:, at:at + P], ident)
                last.then_inc(S["xt_banked"], 1)

            def turn_act():
                e.wait_ge(S["act_ready"], t_.due("act_ready"))
                for k in range(F // P):
                    last = e.transpose(bank[6][:, k * P:(k + 1) * P], act[:, k * P:(k + 1) * P], ident)
                last.then_inc(S["act_banked"], 1)

            def up_half(b, m, h):
                e.wait_ge(S["lo_ready"], t_.due("lo_ready"))
                for c in range(2):
                    k = slice(c * COLS, (c + 1) * COLS)
                    last = three(bank[m][:, :], 2 * h + c, slice(b * P, (b + 1) * P), wh[:, h % CUT, k],
                                 wl[:, h % CUT, k], h + c == 0, h == PART - 1 and c == 1)
                last.then_inc(S["cut_free"], 1)

            def down_half(h):
                if h == 0:
                    e.wait_ge(S["out_ready"], t_.due("out_ready"))
                    e.wait_ge(S["act_lo"], t_.due("act_lo"))
                e.wait_ge(S["lo_ready"], t_.due("lo_ready"))
                k = h // 2
                for c in range(2):
                    r = slice(c * COLS, (c + 1) * COLS)
                    o = bank[2 + 2 * (h % 2) + c][:, :]
                    mm(o, actTh[:, k, :], wh[:, h % CUT, r], start=(k == 0), stop=False)
                    mm(o, actTh[:, k, :], wl[:, h % CUT, r], start=False, stop=False)
                    last = mm(o, actTl[:, k, :], wh[:, h % CUT, r], start=False, stop=(k == 3))
                last.then_inc(S["cut_free"], 1)

            def step(b, first=False, last=False):
                e.wait_ge(S["xt_lo"], t_.due("xt_lo", 2))
                if not first:
                    e.wait_ge(S["silu_ready"], t_.due("silu_ready"))
                for h in range((2 if first else 3) * PART):
                    if h < PART:
                        up_half(b, 0, h)
                    elif h < 2 * PART and not first:
                        down_half(h - PART)
                    else:
                        up_half(b, 1, h % PART)
                    if h == ACT_TURN and not first:
                        turn_act()
                    if h in TURN[first] and not last:
                        turn_gathered(1 - b, TURN[first][h])

            e.sem_inc(S["cut_free"], CUT)
            e.wait_ge(S["start_landed"], 32)
            e.wait_ge(S["router_ready"], 2)
            with t_.layers():
                e.wait_ge(S["rows_ready"], t_.due("rows_ready", NT))
                turn_rows()
                with t_.loop(e.Fori(0, IN_UNITS // RAW // 2)):
                    blocks()

                e.wait_ge(S["f_lo"], t_.due("f_lo"))
                few_columns(4, FPAD, fc, range(NC)).then_inc(S["f_banked"], 1)
                e.wait_ge(S["logf_ready"], t_.due("logf_ready"))
                for t in range(NT):
                    for u in range(t + 1):
                        last = mm(bank[6][:, t * HC:(t + 1) * HC], upto if u == t else ones, logf[:, 2, u, :],
                                  start=(u == 0), stop=(u == t))
                last.then_inc(S["d_banked"], 1)
                e.wait_ge(S["d_ready"], t_.due("d_ready"))
                for t in range(NT):
                    last = e.transpose(bank[6][0:HC, t * P:(t + 1) * P], dcum[:, t, :], ident)
                last.then_inc(S["d_turned"], 1)
                e.wait_ge(S["dT_ready"], t_.due("dT_ready"))
                e.wait_ge(S["head_norms"], t_.due("head_norms"))
                turn(0)
                for i in range(NH + 2):
                    if i < NH:
                        scores(i)
                    if i + 1 < NH:
                        turn(i + 1)
                    if i >= 2:
                        output(i - 2)
                    if 1 <= i <= NH:
                        middle(i - 1)
                e.wait_ge(S["o_ready"], t_.due("o_ready"))

                e.wait_ge(S["mix_scaled"], t_.due("mix_scaled", NT))
                turn_rows()
                with t_.loop(e.Fori(0, OUT_UNITS // RAW // 2)):
                    blocks()

                e.wait_ge(S["rows_ready"], t_.due("rows_ready", NT))
                turn_rows(lambda g: few_columns(0, NE, rt, (2 * g, 2 * g + 1))).then_inc(S["r_banked"], 1)
                e.wait_ge(S["mask_ready"], t_.due("mask_ready"))
                for t in range(NT):
                    for u in range(t + 1):
                        mm(bank[5][:, t * NE:(t + 1) * NE], before if u == t else ones, route[:, 7, u, :],
                           start=(u == 0), stop=(u == t))
                for t in range(NT):
                    last = mm(bank[5][:, NT * NE:(NT + 1) * NE], ones, route[:, 7, t, :],
                              start=(t == 0), stop=(t == NT - 1))
                last.then_inc(S["rank_banked"], 1)

                with t_.one_round():
                    for k in range(NE):
                        e.wait_ge(S["chosen_ready"], t_.due("chosen_ready"))
                        for t in range(NT):
                            last = mm(bank[6][:, 4 * k:4 * k + 4], chosen[:, k % 2, t, :], info[:, t, k, :],
                                      start=(t == 0), stop=(t == NT - 1))
                        last.then_inc(S["slot_banked"], 1)
                    e.wait_ge(S["tables_ready"], t_.due("tables_ready"))
                    for g in range(4):
                        turn_gathered(0, g)
                    step(0, first=True)
                    with t_.loop(e.Fori(0, NE // 2 - 1)):
                        step(1)
                        step(0)
                    step(1, last=True)
                    e.wait_ge(S["silu_ready"], t_.due("silu_ready"))
                    turn_act()
                    for h in range(PART):
                        down_half(h)

        @block.vector
        def _(e):
            v = nc.vector
            t_ = tally(e, start={"cut_free": CUT, "block_out": 2}, tells=False,
                       counted=("hi_ready", "sq_ready", "silu_ready", "xt_hi", "sig_exp", "act_hi", "act_banked",
                                "dve_done"))

            def cut(h):
                e.wait_ge(S["hi_ready"], t_.due("hi_ready"))
                v.tensor_tensor(wl[:, h % CUT, :], raw[:, h // 2 % RAW, h % 2 * HALF:(h % 2 + 1) * HALF],
                                wh[:, h % CUT, :].bitcast(F32), ALU.subtract).then_inc(S["lo_ready"], 1)

            def blocks(n, empty, summed=None):
                def one(behind):
                    for h in range(2 * RAW):
                        cut(h)
                        if h == 3 and behind is not None:
                            empty(*behind)
                        if h == 7 and behind is not None and summed:
                            summed(*behind)
                one(None)
                with t_.loop(e.Fori(0, n // 2 - 1)) as i:
                    one((i * 2, 0))
                    one((i * 2 + 1, 1))
                one((n - 2, 0))
                e.wait_ge(S["cut_free"], t_.due("cut_free", 2 * RAW * n))
                empty(n - 1, 1)
                if summed:
                    summed(n - 1, 1)
                e.wait_ge(S["block_out"], t_.due("block_out", n))

            def refine(n, scale):
                for k, (a, b) in scale.items():
                    last = v.tensor_scalar(stat[:, 0, :, a:b], stat[:, 0, :, a:b], 1.0 / k, EPS,
                                           ALU.mult, ALU.add)
                last.then_inc(S["log_ready"], 1)
                e.wait_ge(S["root_ready"], t_.due("root_ready"))
                ms, y, r = stat[:, 0, :, 0:n], stat[:, 1, :, 0:n], stat[:, 2, :, 0:n]
                v.tensor_tensor(r, y, y, ALU.mult).then_inc(S["dve_done"], 1)
                e.wait_ge(S["dve_done"], t_.due("dve_done"))
                v.tensor_tensor(r, r, ms, ALU.mult).then_inc(S["dve_done"], 1)
                e.wait_ge(S["dve_done"], t_.due("dve_done"))
                v.tensor_scalar(r, r, -0.5, 1.5, ALU.mult, ALU.add).then_inc(S["dve_done"], 1)
                e.wait_ge(S["dve_done"], t_.due("dve_done"))
                v.tensor_tensor(r, r, y, ALU.mult).then_inc(S["dve_done"], 1)
                e.wait_ge(S["dve_done"], t_.due("dve_done"))

            def norm_rows():
                e.wait_ge(S["x_ready"], t_.due("x_ready", NT))
                e.wait_ge(S["gain_landed"], t_.due("gain_landed", 16))
                v.tensor_tensor_reduce(out=rows[:, 1, :], in0=x[:, 1, :], in1=x[:, 1, :], scale=1.0,
                                       scalar=0.0, op0=ALU.mult, op1=ALU.add,
                                       accum_out=stat[:, 0, 1, 0:1]).then_inc(S["dve_done"], 1)
                e.wait_ge(S["dve_done"], t_.due("dve_done"))
                e.wait_ge(S["rows_squared"], t_.due("rows_squared"))
                refine(1, {D: (0, 1)})
                for t in range(NT):
                    v.scalar_tensor_tensor(out=rows[:, t, :], in0=x[:, t, :], scalar=stat[:, 2, t, 0:1],
                                           in1=wide[:, :], op0=ALU.mult, op1=ALU.mult)\
                        .then_inc(S["rows_ready"], 1)
                for g in range(NC // 2):
                    e.wait_ge(S["t_hi"], t_.due("t_hi"))
                    k = slice(2 * g, 2 * g + 2)
                    v.tensor_tensor(xl[:, k, :], bank[4 + g % 4][:, :].rearrange("p (c n) -> p c n", c=2),
                                    xh[:, k, :].bitcast(F32), ALU.subtract).then_inc(S["t_lo"], 1)

            def scaled_heads(ap, r, n):
                view = ap.rearrange("p (h n) -> p h n", h=n)
                width = view.shape[2]
                return v.tensor_tensor(view, view, r.unsqueeze(2).to_broadcast([P, n, width]), ALU.mult)

            e.wait_ge(S["start_landed"], 32)
            e.wait_ge(S["router_ready"], 1)
            v.tensor_tensor(rt[:, :, NE:2 * NE], router_raw, rt[:, :, 0:NE].bitcast(F32), ALU.subtract)\
                .then_inc(S["router_ready"], 1)
            e.wait_ge(S["router_ready"], 2)
            e.wait_ge(S["x_landed"], 16 * NT)
            e.sem_inc(S["lo_ready"], 2 * RAW)
            e.sem_inc(S["block_out"], 2)
            e.sem_inc(S["x_ready"], NT)
            e.sem_inc(S["again_read"], 4)
            e.sem_inc(S["out_ready"], 1)
            e.sem_inc(S["out_free"], 2)

            with t_.layers():
                norm_rows()
                e.wait_ge(S["small_landed"], t_.due("small_landed", 32))
                e.wait_ge(S["f_hi"], t_.due("f_hi"))
                v.tensor_tensor(fc[:, :, FPAD:], fcr[:, :, :], fc[:, :, 0:FPAD].bitcast(F32), ALU.subtract)\
                    .then_inc(S["f_lo"], 1)
                v.tensor_scalar(sml("gqa"), sml("gqa"), 64.0 ** -0.5, None, ALU.mult)
                v.tensor_scalar(sml("gqc"), sml("gqc"), float(HD) ** -0.5, None, ALU.mult)
                v.tensor_scalar(sml("goa"), sml("goa"), sml("rest"), None, ALU.mult)
                vec = sml("lam").rearrange("p (a n) -> p a n", a=4)
                scratch = slots[:, :, :].rearrange("p a b -> p (a b)")
                for k in range(2):
                    ins = v.tensor_tensor_reduce(out=scratch, in0=vec[:, 2 * k, :], in1=vec[:, 2 * k + 1, :],
                                                 scale=1.0, scalar=0.0, op0=ALU.mult, op1=ALU.add,
                                                 accum_out=lam[:, k:k + 1])
                    if k == 0:
                        ins.then_inc(S["dve_done"], 1)
                        e.wait_ge(S["dve_done"], t_.due("dve_done"))
                ins.then_inc(S["lam_dots"], 1)
                e.wait_ge(S["lam_exp"], t_.due("lam_exp"))
                v.tensor_tensor(lam[:, 2:3], lam[:, 0:1], lam[:, 1:2], ALU.subtract).then_inc(S["dve_done"], 1)
                e.wait_ge(S["dve_done"], t_.due("dve_done"))
                v.tensor_tensor(lam[:, 3:4], lam[:, 2:3], sml("init"), ALU.add).then_inc(S["dve_done"], 1)
                e.wait_ge(S["dve_done"], t_.due("dve_done"))
                def to_proj(j, b):
                    for t in range(NT):
                        last = v.tensor_scalar(proj[:, t, bass.ds(j * COLS, COLS)], bank[2 * b + t][:, :],
                                               1.0, None, ALU.mult)
                    last.then_inc(S["block_out"], 1)

                def sum_squares(j, b):
                    e.wait_ge(S["sq_ready"], t_.due("sq_ready"))
                    t_.fence()
                    for t in range(NT):
                        last = v.tensor_reduce(sums[:, t, bass.ds(j * (COLS // 64), COLS // 64)],
                                               rows[:, t, b * COLS:(b + 1) * COLS]
                                               .rearrange("p (h n) -> p h n", n=64), AX, ALU.add)
                    last.then_inc(S["sums_written"], 1)

                blocks(IN_UNITS // 4, to_proj, sum_squares)
                e.wait_ge(S["sums_written"], t_.due("sums_written", IN_UNITS // 4))

                v.tensor_copy(stat[:, 0, :, 0:HALVES_A], sums[:, :, 0:HALVES_A])
                pair = sums[:, :, QC // 64:VC // 64].rearrange("p t (h k) -> p t h k", k=2)
                v.tensor_tensor(stat[:, 0, :, HALVES_A:NORMS], pair[:, :, :, 0], pair[:, :, :, 1], ALU.add)\
                    .then_inc(S["dve_done"], 1)
                e.wait_ge(S["dve_done"], t_.due("dve_done"))
                refine(NORMS, {64: (0, HALVES_A), HD: (HALVES_A, NORMS)})
                for t in range(NT):
                    scaled_heads(proj[:, t, 0:HALVES_A * 64], stat[:, 2, t, 0:HALVES_A], HALVES_A)
                    ins = scaled_heads(proj[:, t, QC:QC + 2 * HC * HD], stat[:, 2, t, HALVES_A:NORMS], 2 * HC)
                ins.then_inc(S["head_norms"], 1)
                e.wait_ge(S["f_banked"], t_.due("f_banked"))
                for t in range(NT):
                    ins = v.tensor_tensor(logf[:, 0, t, :], bank[4 + t][:, 0:HC], sml("bf"), ALU.add)
                ins.then_inc(S["dve_done"], 1)
                e.wait_ge(S["dve_done"], t_.due("dve_done"))
                for t in range(NT):
                    ins = v.tensor_tensor(logf[:, 0, t, :], bank[4 + t][:, FPAD:FPAD + HC], logf[:, 0, t, :],
                                          ALU.add)
                ins.then_inc(S["dve_done"], 1)
                e.wait_ge(S["dve_done"], t_.due("dve_done"))
                v.scalar_tensor_tensor(out=logf[:, 1, :, :], in0=logf[:, 0, :, :], scalar=-1.0,
                                       in1=logf[:, 0, :, :], op0=ALU.mult, op1=ALU.min)\
                    .then_inc(S["f_ready"], 1)
                e.wait_ge(S["f_log"], t_.due("f_log"))
                v.scalar_tensor_tensor(out=logf[:, 2, :, :], in0=logf[:, 0, :, :], scalar=0.0,
                                       in1=logf[:, 1, :, :], op0=ALU.min, op1=ALU.subtract)\
                    .then_inc(S["logf_ready"], 1)


                def key(i):
                    g, _ = HEADS[i]
                    e.wait_ge(S["k_banked"], t_.by("k_banked", i + 1))
                    gain = {"a": sml("gka"), "b": 1.0, "c": sml("gkc")}[g]
                    v.tensor_scalar(qkT[:, i % 2, 1, :], bank[5][:, 0:SEQ], gain, None, ALU.mult)\
                        .then_inc(S["kT_ready"], 1)

                def scores(i):
                    g, h = HEADS[i]
                    b, m = i % 2, i % 3
                    if i >= 2 and HEADS[i - 2][0] == "b":
                        e.wait_ge(S["aT_ready"], t_.by("aT_ready", HEADS[i - 2][1] + 1))
                    if g == "b":
                        z, w = score[:, b, 0, :], score[:, b, 1, :]
                        e.wait_ge(S["z_ready"], t_.due("z_ready"))
                        e.wait_ge(S["soft_ready"], t_.due("soft_ready"))
                        v.scalar_tensor_tensor(out=w, in0=z, scalar=0.0, in1=w, op0=ALU.min,
                                               op1=ALU.subtract).then_inc(S["dve_done"], 1)
                        e.wait_ge(S["dve_done"], t_.due("dve_done"))
                        v.tensor_tensor(z, w, z, ALU.subtract).then_inc(S["dve_done"], 1)
                        e.wait_ge(S["dve_done"], t_.due("dve_done"))
                        v.tensor_tensor(z, z, strict, ALU.mult).then_inc(S["keep_ready"], 1)
                        return
                    e.wait_ge(S["s_banked"], t_.by("s_banked", i + 1))
                    if i >= 2:
                        e.wait_ge(S["m_banked"], t_.by("m_banked", i - 1))
                    ns = 2 if g == "a" else 1
                    if g == "a":
                        slope = 2.0 ** (-8.0 * (h + 1) / HA)
                        for k in range(2):
                            ins = v.scalar_tensor_tensor(out=score[:, b, k, :], in0=cst("ndist"), scalar=slope,
                                                         in1=bank[2 * b + k][:, 0:SPAN], op0=ALU.mult, op1=ALU.add)
                    else:
                        s, lg = score[:, b, 0, :], bank[2 * b]
                        v.scalar_tensor_tensor(out=s[:, 0:P], in0=lg[:, 0:P], scalar=dcum[:, 0, h:h + 1],
                                               in1=cst("causal"), op0=ALU.add, op1=ALU.add)
                        v.tensor_scalar(s[:, P:2 * P], lg[:, P:2 * P], dcum[:, 1, h:h + 1], None, ALU.add)
                        ins = v.scalar_tensor_tensor(out=s[:, 2 * P:SPAN], in0=lg[:, 2 * P:SPAN],
                                                     scalar=dcum[:, 1, h:h + 1], in1=cst("causal"),
                                                     op0=ALU.add, op1=ALU.add)
                    ins.then_inc(S["dve_done"], 1)
                    e.wait_ge(S["dve_done"], t_.due("dve_done"))
                    for t, r in enumerate(ROWS):
                        ins = v.tensor_reduce(soft[:, m, 0, 2 * t:2 * t + ns], score[:, b, 0:ns, r], AX, ALU.max)
                    ins.then_inc(S["dve_done"], 1)
                    e.wait_ge(S["dve_done"], t_.due("dve_done"))
                    v.tensor_scalar(soft[:, m, 1, :] if g == "a" else soft[:, m, 1, 0:3:2],
                                    soft[:, m, 0, :] if g == "a" else soft[:, m, 0, 0:3:2],
                                    -1.0, None, ALU.mult).then_inc(S["neg_max"], 1)
                    e.wait_ge(S["exps_ready"], t_.due("exps_ready"))
                    if g == "c":
                        v.reciprocal(soft[:, m, 3, 0:3:2], soft[:, m, 2, 0:3:2]).then_inc(S["sums_ready"], 1)
                        return
                    v.reciprocal(soft[:, m, 3, :], soft[:, m, 2, :]).then_inc(S["dve_done"], 1)
                    e.wait_ge(S["dve_done"], t_.due("dve_done"))
                    v.tensor_scalar(soft[:, m, 3, 1:4:2], soft[:, m, 3, 1:4:2], lam[:, 3:4], None, ALU.mult)\
                        .then_inc(S["dve_done"], 1)
                    e.wait_ge(S["dve_done"], t_.due("dve_done"))
                    for t, r in enumerate(ROWS):
                        ins = v.tensor_scalar(score[:, b, 1, r], score[:, b, 1, r],
                                              soft[:, m, 3, 2 * t + 1:2 * t + 2], None, ALU.mult)
                    ins.then_inc(S["dve_done"], 1)
                    e.wait_ge(S["dve_done"], t_.due("dve_done"))
                    for t, r in enumerate(ROWS):
                        ins = v.scalar_tensor_tensor(out=score[:, b, 0, r], in0=score[:, b, 0, r],
                                                     scalar=soft[:, m, 3, 2 * t:2 * t + 1],
                                                     in1=score[:, b, 1, r], op0=ALU.mult, op1=ALU.subtract)
                    ins.then_inc(S["weights_ready"], 1)

                def turned(i):
                    g, _ = HEADS[i]
                    b = i % 2
                    if g != "b":
                        return
                    w = score[:, b, 1, :]
                    e.wait_ge(S["m_banked"], t_.by("m_banked", i + 1))
                    v.tensor_tensor(w, w, bank[6][:, 0:SPAN], ALU.add).then_inc(S["sum_ready"], 1)
                    e.wait_ge(S["a_ready"], t_.due("a_ready"))
                    if i >= 2:
                        e.wait_ge(S["o_banked"], t_.by("o_banked", i - 1))
                    v.tensor_tensor(wT[:, b, :], w, strict, ALU.mult).then_inc(S["aT_ready"], 1)

                key(0)
                for i in range(NH + 2):
                    if i + 1 < NH:
                        key(i + 1)
                    if i < NH:
                        scores(i)
                    if 1 <= i <= NH:
                        turned(i - 1)
                e.wait_ge(S["m_banked"], t_.by("m_banked", NH))
                e.sem_inc(S["gain_free"], 1)

                for t in range(NT):
                    e.wait_ge(S["sq_ready"], t_.due("sq_ready"))
                    ins = v.tensor_reduce(stat[:, 0, t, 0:NH],
                                          proj[:, t, 0:D].rearrange("p (h n) -> p h n", n=HD), AX, ALU.add)
                ins.then_inc(S["dve_done"], 1)
                e.wait_ge(S["dve_done"], t_.due("dve_done"))
                refine(NH, {HD: (0, NH)})
                for t in range(NT):
                    scaled_heads(rows[:, t, :], stat[:, 2, t, 0:NH], NH).then_inc(S["mix_scaled"], 1)
                for g in range(NC // 2):
                    e.wait_ge(S["t_hi"], t_.due("t_hi"))
                    for c in (2 * g, 2 * g + 1):
                        gain = sml("goa" if c < HA else "gob" if c < HA + HB else "goc")
                        last = v.scalar_tensor_tensor(out=xl[:, c, :],
                                                      in0=bank[4 + g % 4][:, c % 2 * SEQ:(c % 2 + 1) * SEQ],
                                                      scalar=gain, in1=xh[:, c, :].bitcast(F32),
                                                      op0=ALU.mult, op1=ALU.subtract)
                    last.then_inc(S["t_lo"], 1)

                def to_x(j, b):
                    for t in range(NT):
                        c = bass.ds(j * COLS, COLS)
                        last = v.tensor_tensor(x[:, t, c], bank[2 * b + t][:, :], x[:, t, c], ALU.add)
                    last.then_inc(S["block_out"], 1)

                blocks(OUT_UNITS // 4, to_x)
                e.sem_inc(S["x_ready"], NT)

                norm_rows()
                R = lambda k: route[:, k, :, :]
                G = lambda k: route[:, k, :, :].rearrange("p t (g n) -> p (t g) n", n=EG)

                def over(ap, n):
                    return ap.unsqueeze(2).to_broadcast([P, ap.shape[1], n])

                e.wait_ge(S["r_banked"], t_.due("r_banked"))
                for t in range(NT):
                    ins = v.tensor_copy(route[:, 0, t, :], bank[t][:, NE:2 * NE])
                ins.then_inc(S["dve_done"], 1)
                e.wait_ge(S["dve_done"], t_.due("dve_done"))
                for t in range(NT):
                    ins = v.tensor_tensor(route[:, 0, t, :], bank[t][:, 0:NE], route[:, 0, t, :], ALU.add)
                ins.then_inc(S["r_summed"], 1)
                e.wait_ge(S["r_exp"], t_.due("r_exp"))
                v.tensor_scalar(R(0), R(0), 1.0, None, ALU.add).then_inc(S["dve_done"], 1)
                e.wait_ge(S["dve_done"], t_.due("dve_done"))
                v.reciprocal(R(0), R(0)).then_inc(S["dve_done"], 1)
                e.wait_ge(S["dve_done"], t_.due("dve_done"))
                v.tensor_tensor(R(1), R(0), cst("rbias").unsqueeze(1).to_broadcast([P, NT, NE]), ALU.add)\
                    .then_inc(S["dve_done"], 1)
                e.wait_ge(S["dve_done"], t_.due("dve_done"))
                m = G(1)
                v.tensor_tensor(pairs[:, :, 0:3], m[:, :, 0:1].to_broadcast([P, NT * NG, 3]), m[:, :, 1:4], ALU.add)
                v.tensor_tensor(pairs[:, :, 3:5], m[:, :, 1:2].to_broadcast([P, NT * NG, 2]), m[:, :, 2:4], ALU.add)
                v.tensor_tensor(pairs[:, :, 5:6], m[:, :, 2:3], m[:, :, 3:4], ALU.add).then_inc(S["dve_done"], 1)
                e.wait_ge(S["dve_done"], t_.due("dve_done"))
                v.tensor_reduce(few[:, 0, :], pairs[:, :, :], AX, ALU.max).then_inc(S["dve_done"], 1)
                e.wait_ge(S["dve_done"], t_.due("dve_done"))
                by = lambda k: few[:, k, :].rearrange("p (t g) -> p t g", t=NT)
                v.tensor_reduce(few[:, 1, 0:NT], by(0), AX, ALU.max).then_inc(S["dve_done"], 1)
                e.wait_ge(S["dve_done"], t_.due("dve_done"))
                v.tensor_tensor(by(2), by(0), over(few[:, 1, 0:NT], NG), ALU.is_ge).then_inc(S["dve_done"], 1)
                e.wait_ge(S["dve_done"], t_.due("dve_done"))
                v.tensor_tensor(few[:, 2, :], few[:, 2, :], cst("gcode"), ALU.mult).then_inc(S["dve_done"], 1)
                e.wait_ge(S["dve_done"], t_.due("dve_done"))
                v.tensor_reduce(few[:, 3, 0:NT], by(2), AX, ALU.max).then_inc(S["dve_done"], 1)
                e.wait_ge(S["dve_done"], t_.due("dve_done"))
                v.tensor_tensor(by(2), by(2), over(few[:, 3, 0:NT], NG), ALU.is_equal).then_inc(S["dve_done"], 1)
                e.wait_ge(S["dve_done"], t_.due("dve_done"))
                v.tensor_scalar(few[:, 2, :], few[:, 2, :], BIG, -BIG, ALU.mult, ALU.add).then_inc(S["dve_done"], 1)
                e.wait_ge(S["dve_done"], t_.due("dve_done"))
                v.tensor_tensor(G(2), G(1), over(few[:, 2, :], EG), ALU.add).then_inc(S["dve_done"], 1)
                e.wait_ge(S["dve_done"], t_.due("dve_done"))
                ecode = cst("ecode").rearrange("p (t n) -> p t n", t=NT)
                for k in (4, 5):
                    v.tensor_reduce(few[:, 4, 0:NT], R(2), AX, ALU.max).then_inc(S["dve_done"], 1)
                    e.wait_ge(S["dve_done"], t_.due("dve_done"))
                    v.tensor_tensor(R(3), R(2), over(few[:, 4, 0:NT], NE), ALU.is_ge).then_inc(S["dve_done"], 1)
                    e.wait_ge(S["dve_done"], t_.due("dve_done"))
                    v.tensor_tensor(R(3), R(3), ecode, ALU.mult).then_inc(S["dve_done"], 1)
                    e.wait_ge(S["dve_done"], t_.due("dve_done"))
                    v.tensor_reduce(few[:, 5, 0:NT], R(3), AX, ALU.max).then_inc(S["dve_done"], 1)
                    e.wait_ge(S["dve_done"], t_.due("dve_done"))
                    v.tensor_tensor(R(k), R(3), over(few[:, 5, 0:NT], NE), ALU.is_equal).then_inc(S["dve_done"], 1)
                    e.wait_ge(S["dve_done"], t_.due("dve_done"))
                    if k == 4:
                        v.scalar_tensor_tensor(out=R(2), in0=R(4), scalar=-2.0 * BIG, in1=R(2),
                                               op0=ALU.mult, op1=ALU.add).then_inc(S["dve_done"], 1)
                        e.wait_ge(S["dve_done"], t_.due("dve_done"))
                v.tensor_tensor(R(7), R(4), R(5), ALU.add).then_inc(S["mask_ready"], 1)
                e.wait_ge(S["mask_ready"], t_.due("mask_ready"))
                v.tensor_tensor(R(6), R(0), R(7), ALU.mult).then_inc(S["dve_done"], 1)
                e.wait_ge(S["dve_done"], t_.due("dve_done"))
                v.tensor_reduce(few[:, 4, 0:NT], R(6), AX, ALU.add).then_inc(S["dve_done"], 1)
                e.wait_ge(S["dve_done"], t_.due("dve_done"))
                v.reciprocal(few[:, 5, 0:NT], few[:, 4, 0:NT]).then_inc(S["dve_done"], 1)
                e.wait_ge(S["dve_done"], t_.due("dve_done"))
                token = over(cst("token"), NE)
                v.tensor_copy(info[:, :, :, 0], token)
                v.scalar_tensor_tensor(out=info[:, :, :, 1], in0=R(5), scalar=float(SEQ), in1=token,
                                       op0=ALU.mult, op1=ALU.add)
                v.tensor_copy(info[:, :, :, 3], token)
                v.tensor_tensor(info[:, :, :, 2], R(6), over(few[:, 5, 0:NT], NE), ALU.mult)\
                    .then_inc(S["dve_done"], 1)
                e.wait_ge(S["dve_done"], t_.due("dve_done"))
                e.wait_ge(S["rank_banked"], t_.due("rank_banked"))
                v.scalar_tensor_tensor(out=R(3),
                                       in0=bank[5][:, 0:NT * NE].rearrange("p (t n) -> p t n", t=NT),
                                       scalar=1.0, in1=R(7), op0=ALU.add, op1=ALU.mult).then_inc(S["dve_done"], 1)
                e.wait_ge(S["dve_done"], t_.due("dve_done"))
                v.tensor_copy(left[:, :], bank[5][:, NT * NE:(NT + 1) * NE])
                v.tensor_scalar(R(3), R(3), -1.0, None, ALU.add).then_inc(S["dve_done"], 1)
                e.wait_ge(S["dve_done"], t_.due("dve_done"))

                def rows_lo(b, g):
                    e.wait_ge(S["xt_hi"], t_.due("xt_hi"))
                    k, n = slice(4 * g, 4 * g + 4), slice(b * P, (b + 1) * P)
                    v.tensor_tensor(xl[:, k, n], bank[6 + g % 2][:, :].rearrange("p (c n) -> p c n", c=4),
                                    xh[:, k, n].bitcast(F32), ALU.subtract).then_inc(S["xt_lo"], 1)

                def gated(k):
                    e.wait_ge(S["silu_ready"], t_.due("silu_ready"))
                    v.scalar_tensor_tensor(out=act, in0=act_tmp, scalar=slots[:, bass.ds(k, 1), 2:3]
                                           .rearrange("p a b -> p (a b)"), in1=bank[1][:, :],
                                           op0=ALU.mult, op1=ALU.mult).then_inc(S["act_ready"], 1)

                def act_lo():
                    e.wait_ge(S["act_hi"], t_.due("act_hi"))
                    v.tensor_tensor(actTl[:, :, :], bank[6][:, :].rearrange("p (c n) -> p c n", c=4),
                                    actTh[:, :, :].bitcast(F32), ALU.subtract).then_inc(S["act_lo"], 1)

                def step(b, k, first=False, last=False):
                    for h in range((2 if first else 3) * PART):
                        cut(h)
                        if h == GATED and not first:
                            gated(k - 1)
                        if h == PART and not first:
                            act_lo()
                        if h == SILU + 1:
                            e.wait_ge(S["sig_exp"], t_.due("sig_exp"))
                            v.tensor_scalar(act_tmp, act_tmp, 1.0, None, ALU.add).then_inc(S["dve_done"], 1)
                        if h == SILU + 2:
                            e.wait_ge(S["dve_done"], t_.due("dve_done"))
                            v.reciprocal(act_rec[:, 0:F // 2], act_tmp[:, 0:F // 2])
                        if h == SILU + 3:
                            v.reciprocal(act_rec[:, F // 2:F], act_tmp[:, F // 2:F]).then_inc(S["dve_done"], 1)
                        if h == SILU + 4:
                            e.wait_ge(S["dve_done"], t_.due("dve_done"))
                            v.tensor_tensor(act_tmp, bank[0][:, :], act_rec, ALU.mult)\
                                .then_inc(S["silu_ready"], 1)
                        if h in TURNED[first] and not last:
                            rows_lo(1 - b, TURNED[first][h])

                with t_.one_round():
                    e.wait_ge(S["again_read"], t_.due("again_read", 4))
                    v.tensor_scalar(left[:, :], left[:, :], -float(SLOTS), None, ALU.add).then_inc(S["dve_done"], 1)
                    e.wait_ge(S["dve_done"], t_.due("dve_done"))
                    v.tensor_reduce(more[0:1, 0:1], left[0:1, :], AX, ALU.max).then_inc(S["dve_done"], 1)
                    e.wait_ge(S["dve_done"], t_.due("dve_done"))
                    v.tensor_scalar(again[0:1, 0:1], more[0:1, 0:1], 0.0, None, ALU.is_gt)\
                        .then_inc(S["again_ready"], 1)
                    for k in range(NE):
                        if k >= 2:
                            e.wait_ge(S["slot_banked"], t_.due("slot_banked"))
                        for t in range(NT):
                            last = v.tensor_scalar(chosen[:, k % 2, t, :], cst("slot"), route[:, 3, t, k:k + 1],
                                                   None, ALU.is_equal)
                        last.then_inc(S["chosen_ready"], 1)
                    e.wait_ge(S["slot_banked"], t_.due("slot_banked", 2))
                    v.tensor_copy(slots[:, :, :], bank[6][:, 0:4 * NE].rearrange("p (n k) -> p n k", k=4))\
                        .then_inc(S["dve_done"], 1)
                    e.wait_ge(S["dve_done"], t_.due("dve_done"))
                    v.tensor_scalar(pick[:, 0, :], slots[:, :, 0], 0.0, NOWHERE, ALU.is_equal, ALU.mult)\
                        .then_inc(S["dve_done"], 1)
                    e.wait_ge(S["dve_done"], t_.due("dve_done"))
                    for k, at in ((0, tok_at), (1, put_at)):
                        v.scalar_tensor_tensor(out=at[:, :, 0], in0=slots[:, :, k], scalar=-1.0,
                                               in1=pick[:, 0, :], op0=ALU.add, op1=ALU.add)
                    v.tensor_scalar(R(3), R(3), -float(SLOTS), None, ALU.add).then_inc(S["tables_ready"], 1)
                    e.wait_ge(S["tables_ready"], t_.due("tables_ready"))
                    for g in range(4):
                        rows_lo(0, g)
                    step(0, 0, first=True)
                    with t_.loop(e.Fori(0, NE // 2 - 1)) as i:
                        step(1, i * 2 + 1)
                        step(0, i * 2 + 2)
                    step(1, NE - 1, last=True)
                    for h in range(PART):
                        cut(h)
                        if h == GATED:
                            gated(NE - 1)
                            act_lo()

                for k in range(2):
                    e.wait_ge(S[f"picks_landed{k}"], t_.due(f"picks_landed{k}", 16 * NT))
                    for t in range(NT):
                        ins = v.tensor_tensor(x[:, t, :], x[:, t, :], picked[k * NT + t], ALU.add)
                    ins.then_inc(S["dve_done"], 1)
                    e.wait_ge(S["dve_done"], t_.due("dve_done"))
                e.sem_inc(S["x_ready"], NT)


_INS = ("x", "in_units", "forget_w", "out_units", "expert_units", "norms", "small", "const", "router")


def kernel(x, attn_norm, w_in, b_forget, qnorm_diff, knorm_diff, lam_q1, lam_k1, lam_q2, lam_k2,
           subln_diff, onorm_sb, qnorm_fox, knorm_fox, onorm_fox, w_out, ffn_norm,
           w_router, router_bias, w_gate, w_up, w_down):
    import math

    import concourse.bacc as bacc
    from concourse.bass_utils import run_bass_kernel_spmd as run

    x, w_in, w_out, w_gate, w_up, w_down = (np.asarray(a) for a in (x, w_in, w_out, w_gate, w_up, w_down))
    w_router = np.asarray(w_router)

    def by_columns(w):
        lead, n = w.shape[:-2], w.shape[-1] // COLS
        w = w.reshape(-1, D // (4 * P), 4, P, n, COLS)
        return np.ascontiguousarray(w.transpose(0, 4, 1, 3, 2, 5)).reshape(*lead, n * (D // (4 * P)), P, UNIT)

    gate, up, down = by_columns(w_gate), by_columns(w_up), w_down.reshape(DEPTH, NE, F // P, P, UNIT)
    order = [gate[:, 0], up[:, 0]]
    for k in range(1, NE):
        order += [gate[:, k], down[:, k - 1], up[:, k]]
    experts = np.concatenate(order + [down[:, NE - 1]], 1)
    forget = w_in[:, :, WIN:].reshape(DEPTH, NC, P, HC).transpose(0, 2, 1, 3)
    forget = np.concatenate([forget, np.zeros((DEPTH, P, NC, FPAD - HC), np.float32)], 3)
    small = np.zeros((DEPTH, P, SMALL), np.float32)

    def put(name, a):
        small[:, :, SM[name][0]:SM[name][1]] = a

    for name, a, times in (("gqa", qnorm_diff, 2), ("gka", knorm_diff, 2), ("gqc", qnorm_fox, 1),
                           ("gkc", knorm_fox, 1), ("goa", subln_diff, 1), ("gob", onorm_sb, 1),
                           ("goc", onorm_fox, 1)):
        put(name, np.tile(np.asarray(a), (1, times))[:, :, None])
    put("bf", np.asarray(b_forget)[:, None, :])
    put("lam", np.concatenate([np.asarray(a) for a in (lam_q1, lam_k1, lam_q2, lam_k2)], 1)[:, None, :])
    init = np.array([0.8 - 0.6 * math.exp(-0.3 * k) for k in range(DEPTH)])
    put("init", init[:, None, None])
    put("rest", (1.0 - init)[:, None, None])
    const = shape_constants()
    const[:, CN["rbias"][0]:CN["rbias"][1]] = np.asarray(router_bias)[None, :]
    arrays = dict(zip(_INS, (
        x.reshape(SEQ, D), by_columns(w_in[:, :, :WIN]).reshape(-1, P, UNIT), forget,
        by_columns(w_out).reshape(-1, P, UNIT), experts.reshape(-1, P, UNIT),
        np.stack([np.asarray(attn_norm), np.asarray(ffn_norm)], 1).reshape(2 * DEPTH, D), small, const,
        w_router.reshape(NC, P, NE).transpose(1, 0, 2))))
    arrays = {f"in_{k}": np.ascontiguousarray(a) for k, a in arrays.items()}

    nc = bacc.Bacc("TRN2", target_bir_lowering=False, num_devices=1)
    args = [nc.dram_tensor(k, a.shape, mybir.dt.from_np(a.dtype), kind="ExternalInput").ap()
            for k, a in arrays.items()]
    rows_dram = nc.dram_tensor("expert_rows", (SEQ, D), F32, kind="Internal").ap()
    picks_dram = nc.dram_tensor("picks", (2 * SEQ, D), F32, kind="Internal").ap()
    out = nc.dram_tensor("out_rows", (SEQ, D), F32, kind="ExternalOutput").ap()
    trunk(nc, *args, rows_dram, picks_dram, out)
    r = run(nc, [arrays], core_ids=[0])
    return r.results[0]["out_rows"].reshape(1, SEQ, D)
```
